# Optimizing a Trainium2 kernel written in Bass

```python
import math
import jax, jax.numpy as jnp
from jax import lax
import numpy as np

D_MODEL = 1024
BATCH = 1
SEQ = 512
DEPTH = 2
DEC_BATCH = 8
DEC_SEQ = 1
PAST_LEN = 4096
PAGE_SIZE = 128

N_A_LAYERS = DEPTH // 2
N_B_LAYERS = DEPTH - N_A_LAYERS
N_DENSE = (DEPTH + 1) // 2
N_MOE = DEPTH // 2
DN_HEADS = 6
DN_DK = 128
DN_DV = 128
DN_QK_DIM = DN_HEADS * DN_DK
DN_V_DIM = DN_HEADS * DN_DV
CONV_W = 4
CONV_DIM = 2 * DN_QK_DIM + DN_V_DIM
CHUNK = 64
MLA_HEADS = 6
Q_LORA = 384
KV_LORA = 256
QK_NOPE = 128
QK_ROPE = 64
V_HEAD = 128
ROPE_THETA = 10000.0
Q_BLOCK = 128
MLA_SCALE = (QK_NOPE + QK_ROPE) ** -0.5
N_MEM = 256
MEM_HEADS = 4
MEM_HD = 64
MEM_DIM = MEM_HEADS * MEM_HD
MIX_WIDTH = DN_V_DIM + MEM_DIM
IN_A = CONV_DIM + DN_V_DIM + 2 * DN_HEADS + MEM_DIM
IN_B = Q_LORA + MEM_DIM
D_FF = 2816
N_EXPERTS = 8
TOP_K = 2
D_FF_E = 1408
EPS = 1e-6

kernel_name = "yoco_gdn_mla_memory_decoder_step"

F32 = jnp.float32

def rmsnorm(x, g):
    xf = x.astype(F32)
    y = xf * lax.rsqrt(jnp.mean(xf * xf, -1, keepdims=True) + EPS)
    return (y * g.astype(F32)).astype(x.dtype)

def l2norm(x):
    xf = x.astype(F32)
    return (xf * lax.rsqrt(jnp.sum(xf * xf, -1, keepdims=True) + EPS)).astype(x.dtype)

def rope(x, pos):
    half = x.shape[-1] // 2
    inv = ROPE_THETA ** (-jnp.arange(half, dtype=F32) / half)
    ang = pos.astype(F32)[:, None] * inv[None, :]
    shp = (1, pos.shape[0]) + (1,) * (x.ndim - 3) + (half,)
    cos = jnp.cos(ang).reshape(shp)
    sin = jnp.sin(ang).reshape(shp)
    x1 = x[..., :half].astype(F32)
    x2 = x[..., half:].astype(F32)
    return jnp.concatenate([x1 * cos - x2 * sin, x1 * sin + x2 * cos], -1).astype(x.dtype)

def short_conv(u, prev, w):
    S = u.shape[1]
    up = jnp.concatenate([prev.astype(u.dtype), u], 1)
    y = up[:, 0:S] * w[0]
    for j in range(1, CONV_W):
        y = y + up[:, j:j + S] * w[j]
    return jax.nn.silu(y), up[:, -(CONV_W - 1):]

def gated_delta_rule(q, k, v, g, beta, s0):
    B, S, H, DK = q.shape
    DV = v.shape[-1]
    C = CHUNK
    pad = (-S) % C

    def prep(t):
        t = t.astype(F32)
        t = jnp.pad(t, [(0, 0), (0, pad)] + [(0, 0)] * (t.ndim - 2))
        n = t.shape[1] // C
        t = t.reshape((B, n, C) + t.shape[2:])
        return jnp.moveaxis(t, 3, 1)

    qc, kc, vc, gc, bc = (prep(q.astype(F32) * DK ** -0.5), prep(k), prep(v), prep(g), prep(beta))
    gcum = jnp.cumsum(gc, -1)
    tri = jnp.tril(jnp.ones((C, C), bool))
    eye = jnp.eye(C, dtype=F32)
    decay = jnp.exp(jnp.where(tri, gcum[..., :, None] - gcum[..., None, :], -jnp.inf))
    kb = kc * bc[..., None]
    vb = vc * bc[..., None]
    lower = jnp.einsum('bhnid,bhnjd->bhnij', kb, kc) * decay * (1.0 - eye)
    rhs = jnp.concatenate([vb, kb * jnp.exp(gcum)[..., None]], -1)
    sol = lax.linalg.triangular_solve(eye + lower, rhs, left_side=True, lower=True, unit_diagonal=True)
    u = sol[..., :DV]
    w = sol[..., DV:]
    qk = jnp.einsum('bhnid,bhnjd->bhnij', qc, kc) * decay
    q_g = qc * jnp.exp(gcum)[..., None]
    g_last = gcum[..., -1]
    k_g = kc * jnp.exp(g_last[..., None] - gcum)[..., None]

    def step(st, inp):
        qk_n, qg_n, w_n, u_n, kg_n, gl_n = inp
        v_new = u_n - jnp.einsum('bhcd,bhde->bhce', w_n, st)
        o = jnp.einsum('bhcd,bhde->bhce', qg_n, st) + jnp.einsum('bhij,bhje->bhie', qk_n, v_new)
        st = st * jnp.exp(gl_n)[..., None, None] + jnp.einsum('bhcd,bhce->bhde', kg_n, v_new)
        return st, o

    xs = tuple(jnp.moveaxis(t, 2, 0) for t in (qk, q_g, w, u, k_g, g_last))
    s_fin, o = lax.scan(step, s0.astype(F32), xs)
    n = o.shape[0]
    o = jnp.moveaxis(o, 0, 2).reshape(B, H, n * C, DV)[:, :, :S]
    return jnp.transpose(o, (0, 2, 1, 3)).astype(v.dtype), s_fin

def deltanet_mixer(h, w_in, conv_w, a_log, dt_bias, g_onorm, conv_prev, s_prev):
    B, S, _ = h.shape
    proj = h @ w_in
    o1 = CONV_DIM
    o2 = o1 + DN_V_DIM
    o3 = o2 + DN_HEADS
    o4 = o3 + DN_HEADS
    qkv, conv_new = short_conv(proj[..., :o1], conv_prev, conv_w)
    z = proj[..., o1:o2].reshape(B, S, DN_HEADS, DN_DV)
    b = proj[..., o2:o3]
    a = proj[..., o3:o4]
    mq = proj[..., o4:]
    q = l2norm(qkv[..., :DN_QK_DIM].reshape(B, S, DN_HEADS, DN_DK))
    k = l2norm(qkv[..., DN_QK_DIM:2 * DN_QK_DIM].reshape(B, S, DN_HEADS, DN_DK))
    v = qkv[..., 2 * DN_QK_DIM:].reshape(B, S, DN_HEADS, DN_DV)
    beta = jax.nn.sigmoid(b.astype(F32))
    g = -jnp.exp(a_log.astype(F32)) * jax.nn.softplus(a.astype(F32) + dt_bias.astype(F32))
    o, s_new = gated_delta_rule(q, k, v, g, beta, s_prev)
    o = rmsnorm(o, g_onorm) * jax.nn.silu(z)
    return o.reshape(B, S, DN_V_DIM), mq, conv_new, s_new.astype(s_prev.dtype)

def shared_latent_kv(x, pos, g_kv, w_kv_a, g_ckv):
    kv = rmsnorm(x, g_kv) @ w_kv_a
    ckv = rmsnorm(kv[..., :KV_LORA], g_ckv)
    kpe = rope(kv[..., KV_LORA:], pos)
    return ckv, kpe

def mla_prompt_attend(q_lat, q_pe, ckv, kpe):
    B, S, H, C = q_lat.shape
    nb = S // Q_BLOCK
    kpos = jnp.arange(S)

    def blk(i):
        ql = lax.dynamic_slice_in_dim(q_lat, i * Q_BLOCK, Q_BLOCK, 1)
        qp = lax.dynamic_slice_in_dim(q_pe, i * Q_BLOCK, Q_BLOCK, 1)
        s = (jnp.einsum('bqhc,bkc->bhqk', ql, ckv).astype(F32)
             + jnp.einsum('bqhr,bkr->bhqk', qp, kpe).astype(F32)) * MLA_SCALE
        qpos = i * Q_BLOCK + jnp.arange(Q_BLOCK)
        s = jnp.where(kpos[None, :] <= qpos[:, None], s, -jnp.inf)
        p = jax.nn.softmax(s, -1).astype(ckv.dtype)
        return jnp.einsum('bhqk,bkc->bqhc', p, ckv)

    o = lax.map(blk, jnp.arange(nb))
    return jnp.moveaxis(o, 0, 1).reshape(B, S, H, C)

def mla_sample_attend(q_lat, q_pe, ckv_past, kpe_past, ckv_new, kpe_new):
    Sd = q_lat.shape[1]
    P = ckv_past.shape[1]
    s_past = (jnp.einsum('bqhc,bkc->bhqk', q_lat, ckv_past).astype(F32)
              + jnp.einsum('bqhr,bkr->bhqk', q_pe, kpe_past).astype(F32))
    s_new = (jnp.einsum('bqhc,bkc->bhqk', q_lat, ckv_new).astype(F32)
             + jnp.einsum('bqhr,bkr->bhqk', q_pe, kpe_new).astype(F32))
    s_new = jnp.where(jnp.tril(jnp.ones((Sd, Sd), bool)), s_new, -jnp.inf)
    p = jax.nn.softmax(jnp.concatenate([s_past, s_new], -1) * MLA_SCALE, -1).astype(ckv_past.dtype)
    return (jnp.einsum('bhqk,bkc->bqhc', p[..., :P], ckv_past)
            + jnp.einsum('bhqk,bkc->bqhc', p[..., P:], ckv_new))

def mla_mixer(h, pos, ckv, kpe, w_in, g_ql, w_qb, w_uk, w_uv, attend):
    B, S, _ = h.shape
    proj = h @ w_in
    ql = proj[..., :Q_LORA]
    mq = proj[..., Q_LORA:]
    qf = (rmsnorm(ql, g_ql) @ w_qb).reshape(B, S, MLA_HEADS, QK_NOPE + QK_ROPE)
    q_pe = rope(qf[..., QK_NOPE:], pos)
    q_lat = jnp.einsum('bshn,chn->bshc', qf[..., :QK_NOPE], w_uk)
    o_lat = attend(q_lat, q_pe, ckv, kpe)
    o = jnp.einsum('bshc,chv->bshv', o_lat, w_uv).reshape(B, S, MLA_HEADS * V_HEAD)
    return o, mq

def memory_kv(mem, g_mem, w_mem_kv):
    B, M, _ = mem.shape
    L = g_mem.shape[0]
    mf = mem.astype(F32)
    mn = (mf * lax.rsqrt(jnp.mean(mf * mf, -1, keepdims=True) + EPS)).astype(mem.dtype)
    kv = jnp.einsum('bmd,ld,lde->lbme', mn, g_mem, w_mem_kv)
    k = kv[..., :MEM_DIM].reshape(L, B, M, MEM_HEADS, MEM_HD)
    v = kv[..., MEM_DIM:].reshape(L, B, M, MEM_HEADS, MEM_HD)
    return k, v

def mem_attend(mq, mk, mv):
    B, S, _ = mq.shape
    q = mq.reshape(B, S, MEM_HEADS, MEM_HD)
    s = jnp.einsum('bqhd,bkhd->bhqk', q, mk.astype(q.dtype)).astype(F32) * MEM_HD ** -0.5
    p = jax.nn.softmax(s, -1).astype(q.dtype)
    return jnp.einsum('bhqk,bkhd->bqhd', p, mv.astype(q.dtype)).reshape(B, S, MEM_DIM)

def swiglu(h, wg, wu, wd):
    return (jax.nn.silu(h @ wg) * (h @ wu)) @ wd

def moe(h, w_router, wg, wu, wd):
    probs = jax.nn.softmax((h @ w_router).astype(F32), -1)
    top_p, top_i = lax.top_k(probs, TOP_K)
    top_p = top_p / jnp.sum(top_p, -1, keepdims=True)
    gates = jnp.sum(jax.nn.one_hot(top_i, N_EXPERTS, dtype=F32) * top_p[..., None], -2).astype(h.dtype)
    out = jnp.zeros_like(h)
    for e in range(N_EXPERTS):
        out = out + gates[..., e:e + 1] * swiglu(h, wg[e], wu[e], wd[e])
    return out

def run_trunk(x, pos, mem_k, mem_v, conv_prev, dn_prev, attend_b, P):
    conv_states, dn_states = [], []
    ckv = None
    kpe = None
    for l in range(DEPTH):
        if l == N_A_LAYERS:
            ckv, kpe = shared_latent_kv(x, pos, P['g_kv'], P['w_kv_a'], P['g_ckv'])
        h = rmsnorm(x, P['g_mix'][l])
        if l < N_A_LAYERS:
            o_tok, mq, c_new, s_new = deltanet_mixer(h, P['w_in_a'][l], P['conv_w'][l], P['a_log'][l],
                                                     P['dt_bias'][l], P['g_onorm'][l], conv_prev[l], dn_prev[l])
            conv_states.append(c_new)
            dn_states.append(s_new)
        else:
            j = l - N_A_LAYERS
            o_tok, mq = mla_mixer(h, pos, ckv, kpe, P['w_in_b'][j], P['g_qlora'][j], P['w_q_b'][j],
                                  P['w_uk'], P['w_uv'], attend_b)
        o_mem = mem_attend(mq, mem_k[l], mem_v[l])
        x = x + jnp.concatenate([o_tok, o_mem], -1) @ P['w_out'][l]
        h = rmsnorm(x, P['g_ffn'][l])
        i = l // 2
        if l % 2 == 0:
            x = x + swiglu(h, P['w_gate'][i], P['w_up'][i], P['w_down'][i])
        else:
            x = x + moe(h, P['w_router'][i], P['we_gate'][i], P['we_up'][i], P['we_down'][i])
    y = rmsnorm(x, P['g_final'])
    return y, jnp.stack(conv_states), jnp.stack(dn_states), ckv, kpe

def setup_inputs(seed: int = 0) -> dict:
    key = jax.random.key(seed)
    ks = iter(jax.random.split(key, 64))

    def nrm(shape, scale):
        return jax.random.normal(next(ks), shape, F32) * scale

    def gain(shape):
        return 1.0 + nrm(shape, 0.02)

    n_pages = PAST_LEN // PAGE_SIZE
    n_used = DEC_BATCH * n_pages
    n_pool = n_used + n_used // 4
    inp = {}
    inp['x_prompt'] = nrm((BATCH, SEQ, D_MODEL), 1.0)
    inp['x_sample'] = nrm((DEC_BATCH, DEC_SEQ, D_MODEL), 1.0)
    inp['cache_mem_k'] = nrm((DEPTH, DEC_BATCH, N_MEM, MEM_HEADS, MEM_HD), 1.0)
    inp['cache_mem_v'] = nrm((DEPTH, DEC_BATCH, N_MEM, MEM_HEADS, MEM_HD), 1.0)
    inp['cache_ckv'] = nrm((n_pool, PAGE_SIZE, KV_LORA), 1.0)
    inp['cache_kpe'] = nrm((n_pool, PAGE_SIZE, QK_ROPE), 1.0)
    inp['state_delta'] = nrm((N_A_LAYERS, DEC_BATCH, DN_HEADS, DN_DK, DN_DV), 0.1)
    inp['state_conv'] = nrm((N_A_LAYERS, DEC_BATCH, CONV_W - 1, CONV_DIM), 1.0)
    inp['page_table'] = jax.random.permutation(next(ks), n_pool)[:n_used].reshape(DEC_BATCH, n_pages).astype(jnp.int32)
    inp['mem_prompt'] = nrm((BATCH, N_MEM, D_MODEL), 1.0)
    inp['g_mix'] = gain((DEPTH, D_MODEL))
    inp['g_ffn'] = gain((DEPTH, D_MODEL))
    inp['g_final'] = gain((D_MODEL,))
    inp['w_in_a'] = nrm((N_A_LAYERS, D_MODEL, IN_A), D_MODEL ** -0.5)
    inp['conv_w'] = nrm((N_A_LAYERS, CONV_W, CONV_DIM), CONV_W ** -0.5)
    inp['a_log'] = jnp.log(jax.random.uniform(next(ks), (N_A_LAYERS, DN_HEADS), F32, 1.0, 16.0))
    dt = jnp.exp(jax.random.uniform(next(ks), (N_A_LAYERS, DN_HEADS), F32, math.log(1e-3), math.log(1e-1)))
    inp['dt_bias'] = dt + jnp.log(-jnp.expm1(-dt))
    inp['g_onorm'] = gain((N_A_LAYERS, DN_DV))
    inp['w_in_b'] = nrm((N_B_LAYERS, D_MODEL, IN_B), D_MODEL ** -0.5)
    inp['g_qlora'] = gain((N_B_LAYERS, Q_LORA))
    inp['w_q_b'] = nrm((N_B_LAYERS, Q_LORA, MLA_HEADS * (QK_NOPE + QK_ROPE)), Q_LORA ** -0.5)
    inp['g_kv'] = gain((D_MODEL,))
    inp['w_kv_a'] = nrm((D_MODEL, KV_LORA + QK_ROPE), D_MODEL ** -0.5)
    inp['g_ckv'] = gain((KV_LORA,))
    inp['w_uk'] = nrm((KV_LORA, MLA_HEADS, QK_NOPE), KV_LORA ** -0.5)
    inp['w_uv'] = nrm((KV_LORA, MLA_HEADS, V_HEAD), KV_LORA ** -0.5)
    inp['g_mem'] = gain((DEPTH, D_MODEL))
    inp['w_mem_kv'] = nrm((DEPTH, D_MODEL, 2 * MEM_DIM), D_MODEL ** -0.5)
    inp['w_out'] = nrm((DEPTH, MIX_WIDTH, D_MODEL), MIX_WIDTH ** -0.5)
    inp['w_gate'] = nrm((N_DENSE, D_MODEL, D_FF), D_MODEL ** -0.5)
    inp['w_up'] = nrm((N_DENSE, D_MODEL, D_FF), D_MODEL ** -0.5)
    inp['w_down'] = nrm((N_DENSE, D_FF, D_MODEL), D_FF ** -0.5)
    inp['w_router'] = nrm((N_MOE, D_MODEL, N_EXPERTS), D_MODEL ** -0.5)
    inp['we_gate'] = nrm((N_MOE, N_EXPERTS, D_MODEL, D_FF_E), D_MODEL ** -0.5)
    inp['we_up'] = nrm((N_MOE, N_EXPERTS, D_MODEL, D_FF_E), D_MODEL ** -0.5)
    inp['we_down'] = nrm((N_MOE, N_EXPERTS, D_FF_E, D_MODEL), D_FF_E ** -0.5)
    return inp

def reference(x_prompt, x_sample, cache_mem_k, cache_mem_v, cache_ckv, cache_kpe, state_delta, state_conv,
              page_table, mem_prompt, g_mix, g_ffn, g_final, w_in_a, conv_w, a_log, dt_bias, g_onorm,
              w_in_b, g_qlora, w_q_b, g_kv, w_kv_a, g_ckv, w_uk, w_uv, g_mem, w_mem_kv, w_out,
              w_gate, w_up, w_down, w_router, we_gate, we_up, we_down):
    P = dict(g_mix=g_mix, g_ffn=g_ffn, g_final=g_final, w_in_a=w_in_a, conv_w=conv_w, a_log=a_log,
             dt_bias=dt_bias, g_onorm=g_onorm, w_in_b=w_in_b, g_qlora=g_qlora, w_q_b=w_q_b, g_kv=g_kv,
             w_kv_a=w_kv_a, g_ckv=g_ckv, w_uk=w_uk, w_uv=w_uv, w_out=w_out, w_gate=w_gate, w_up=w_up,
             w_down=w_down, w_router=w_router, we_gate=we_gate, we_up=we_up, we_down=we_down)
    bp, sp, _ = x_prompt.shape
    p_mem_k, p_mem_v = memory_kv(mem_prompt, g_mem, w_mem_kv)
    conv0 = jnp.zeros((N_A_LAYERS, bp, CONV_W - 1, CONV_DIM), x_prompt.dtype)
    s0 = jnp.zeros((N_A_LAYERS, bp, DN_HEADS, DN_DK, DN_DV), x_prompt.dtype)
    y_prompt, p_conv, p_delta, p_ckv, p_kpe = run_trunk(x_prompt, jnp.arange(sp), p_mem_k, p_mem_v,
                                                        conv0, s0, mla_prompt_attend, P)
    nb, npg = page_table.shape
    past = npg * PAGE_SIZE
    ckv_past = cache_ckv[page_table].reshape(nb, past, KV_LORA)
    kpe_past = cache_kpe[page_table].reshape(nb, past, QK_ROPE)

    def attend_sample(q_lat, q_pe, ckv_new, kpe_new):
        return mla_sample_attend(q_lat, q_pe, ckv_past, kpe_past, ckv_new, kpe_new)

    pos_s = past + jnp.arange(x_sample.shape[1])
    y_sample, s_conv, s_delta, s_ckv, s_kpe = run_trunk(x_sample, pos_s, cache_mem_k, cache_mem_v,
                                                        state_conv, state_delta, attend_sample, P)
    return (y_prompt, y_sample, p_delta, p_conv, p_ckv, p_kpe, p_mem_k, p_mem_v, s_delta, s_conv, s_ckv, s_kpe)


_drawn_inputs = setup_inputs


def setup_inputs(seed=0):
    import zlib

    import numpy as np

    out = dict(_drawn_inputs(seed))
    spreads = {}
    factors = {'cache_ckv': 2.997,
     'g_final': 2.89,
     'g_onorm': 3.035,
     'g_qlora': 7.375,
     'g_kv': 2.688,
     'g_ckv': 2.718,
     'g_mem': 2.869}
    for name, (base, spread) in spreads.items():
        noise = np.random.default_rng([zlib.crc32(name.encode()), seed]).standard_normal(out[name].shape)
        drawn = base * np.exp(spread * noise) if base else spread * noise
        out[name] = __import__('jax').numpy.asarray(drawn.astype(out[name].dtype))
    for name, factor in factors.items():
        out[name] = (out[name] * factor).astype(out[name].dtype)
    return out
```

```python
from contextlib import ExitStack

import concourse.bass as bass
from concourse import mybir

F32 = mybir.dt.float32
U8 = mybir.dt.uint8
I32 = mybir.dt.int32
ALU = mybir.AluOpType
ACT = mybir.ActivationFunctionType
X = mybir.AxisListType.X

P = 128
D = 1024
KT = D // P
S = 512
NB = 8
T = S + NB
HALF = T // 2
HALVES = [(0, HALF), (HALF, T)]
NT = S // P
H = 6
HD = 128
CW = 4
QKV = 3 * H
CONV = QKV * HD
IN_A = CONV + H * HD + 2 * H + 256
MEM = 256
MH = 4
MD = 64
QL = 384
KV = 256
ROPE = 64
QH = HD + ROPE
QHP = KV + ROPE
FE = 1408
FB = FE // P
DENSE_PARTS = 2
NE = 8
PAGES = 32
GP = 8
NG = PAGES // GP
PAIRS = NB * PAGES // 2
SP_PAIRS = PAGES // 2
PSLOTS = 8
AHEAD = 2
LAG = 6
EXPERT_USES = [6, 5, 6, 5, 4, 4, 6, 6]
EPS = 1e-6
MLA_SCALE = QH ** -0.5
MEM_SCALE = MD ** -0.5
WS = 11
DS = 4
UW = 3 + S + NB * CW
CONVW = UW - 3
LEVELS = 7
SEL = 2 * H
NORM_MIX0, NORM_FFN0, NORM_KV, NORM_MIX1, NORM_FFN1, NORM_FINAL = range(6)
GAIN = {NORM_MIX0: 0, NORM_MIX1: 1, NORM_FFN0: 2, NORM_FFN1: 3, NORM_FINAL: 4, NORM_KV: 5}
GAIN_MEM = 6
SLOTS = 176
ROWS = SLOTS // 2
PASSES = (2 * T + NE * (SLOTS - 1)) // SLOTS
ZROWS = -(-(PASSES + 1) * SLOTS // P)
ZFILL = 4
ZCOLS = 256
NGAIN = 8
NEG = -1e30


def build(nc, a, o):
    (y_prompt, y_sample, p_delta, p_conv, p_ckv, p_kpe, p_mem_k, p_mem_v, s_delta, s_conv, s_ckv, s_kpe) = o
    with ExitStack() as ctx:
        def sb(name, shape, dt=F32):
            return ctx.enter_context(nc.sbuf_tensor(name, shape, dt))[:]

        def sem(name):
            return ctx.enter_context(nc.semaphore(name))

        slots = nc.dram_tensor("slots", (ZROWS * P, D), F32).ap()

        xT = sb("xT", [P, KT, T])
        hT = sb("hT", [P, KT, T])
        w_ring = sb("w_ring", [P, WS, KT, P])
        memkT = sb("memkT", [P, 2, 2, MEM])
        memv = sb("memv", [P, 2, 2, MEM])
        CF = sb("CF", [P, 5 * P + NE + PASSES + 1])
        order = CF[:, 5 * P:5 * P + NE]
        numbers = CF[:, 5 * P + NE:-1]
        run = CF[:, 5 * P + NE + PASSES:]
        ident, ones, incl, cmask, rotT = (CF[:, i * P:(i + 1) * P] for i in range(5))
        sel = sb("sel", [SEL, SEL, P])
        gains = sb("gains", [P, KT, NGAIN])
        convw = sb("convw", [P, QKV, 28])
        cnew = sb("cnew", [P, QKV, 11])
        g_on = sb("g_on", [P, 1])
        g_ql = sb("g_ql", [P, 3])
        g_ck = sb("g_ck", [P, 2])
        page_rows = sb("page_rows", [P, NB * NG], I32)
        page_f = sb("page_f", [P, NB * NG])
        alog = sb("alog", [P, H])
        dtb = sb("dtb", [P, H])
        epst = sb("epst", [P, 2])
        wba = sb("wba", [P, KT, 2 * H])
        wrt = sb("wrt", [P, KT, NE])
        rstd = sb("rstd", [P, T])
        mqst = sb("mqst", [P, MEM])
        Pm32 = sb("Pm32", [P, MEM])
        pvs = Pm32
        vnt = sb("vnt", [P, P])
        small = sb("small", [P, 1150])
        taken = [0]

        def bit(*shape):
            n = 1
            for k in shape:
                n *= k
            v = small[:, taken[0]:taken[0] + n]
            taken[0] += n
            if len(shape) == 2:
                v = v.rearrange("p (a b) -> p a b", a=shape[0])
            if len(shape) == 3:
                v = v.rearrange("p (a b c) -> p a b c", a=shape[0], b=shape[1])
            return v

        GB, A1, AB, E1, EB = bit(5, 2 * H), bit(5, H), bit(5, H), bit(5, H), bit(5, H)
        EA, gg, BG = bit(H), bit(5, H), bit(5, 2 * H)
        egc, begc, kgs, kgt, glx = bit(NT, H), bit(NT, H), bit(H, NT), bit(NT), bit(H, NT)
        bsamp, egs, qkp, qkd, vs = bit(2 * H, NB), bit(H, NB), bit(H, NB), bit(H, NB), bit(H, NB)
        sa, sbb = bit(NB), bit(NB)
        assert taken[0] < 830
        taken[0] = shared = 830
        mmax, msum = bit(MH, 2, 2), bit(MH, 2, 2)
        msc, pT = bit(2, NB * MH), bit(2, NB * MH)
        m32, s32 = bit(1), bit(1)
        memss = bit(2)
        taken[0] = 0
        ownp, own, pmax, pmx, pdiag = bit(3, NB * H), bit(NB * H), bit(H), bit(1), bit(H)
        psums, mxb, exn2, tot2, ownv = bit(H), bit(H), bit(2, H), bit(2, H), bit(2, NB)
        olat, otmp = bit(2, NB * H), bit(2, H)
        lg, lgm, lgs, chosen = bit(5, NE), bit(5), bit(5), bit(5, NE)
        eq, oh, oh2, tv = bit(5, NE), bit(5, NE), bit(5, NE), bit(5)
        top1, top2 = bit(5), bit(5)
        atmax, atsum = bit(H, NT), bit(H, NT)
        assert taken[0] <= shared, taken
        taken[0] = 0
        npass, upto1, upto2, first = bit(NE), bit(4 + NE), bit(4 + NE), bit(NE)
        place_of, slotf = bit(5, NE), bit(2, 5)
        slot = bit(2, 5).bitcast(I32)
        cmp, tabf = bit(PASSES, NE), bit(PASSES + 1)
        table = bit(PASSES + 1).bitcast(I32)
        outss = bit(5)
        assert taken[0] <= 600
        BGT = rstd[0:2 * H, :]
        arena_bytes = 102960
        arena = sb("arena", [P, arena_bytes // 4])

        def place(at, *shape):
            n = 1
            for s in shape:
                n *= s
            assert at % 4 == 0 and at + 4 * n <= arena_bytes, (at, shape)
            v = arena[:, at // 4:at // 4 + n]
            if len(shape) == 2:
                v = v.rearrange("p (a b) -> p a b", a=shape[0])
            if len(shape) == 3:
                v = v.rearrange("p (a b c) -> p a b c", a=shape[0], b=shape[1])
            return v, at + 4 * n

        xtok, q = place(0, 5, D)
        gtok, q = place(q, D)
        cvtok, q = place(q, CONV)
        mtok, q = place(q, 2, D)
        mnT, q = place(q, 2, KT, MEM)
        mscr, q = place(q, D)
        kvT, q = place(q, 2, 4, MEM)
        mkt, q = place(q, 2, 2, MEM)

        qkv, q = place(0, QKV, T)
        zs, q = place(q, H, T)
        mq0, q = place(q, 2, T)
        gdn0 = q
        U, q = place(q, 2, UW + 1)
        Y, q = place(q, 2, CONVW)
        Einv, q = place(gdn0, 3, S)
        nWT, q = place(q, 3, S)
        QKT, q = place(q, 3, S)
        LT, q = place(q, 3, S)
        Dinv, q = place(q, 3, S)
        Xs, q = place(q, 3, S)
        cout, _ = place(q, 2, 512)
        EG, q = place(q, S)
        DT, q = place(q, S)
        t1, _ = place(q, S)
        kbg, q = place(q, S)
        vn, q = place(q, 3, P)
        St, q = place(q, 3, P)
        lmw, q = place(q, 2 * LEVELS * P // 4)
        lmask = lmw.bitcast(U8).rearrange("p (l j) -> p l j", l=2 * LEVELS)
        sqb, q = place(gdn0, 2, T)
        nrb, q = place(q, 2, T)
        Ssb, q = place(q, 2, NB * P)
        ktok, q = place(q, H * P)
        kmask, q = place(q, NB, P)

        d_ring, q = place(arena_bytes // 4 * 4 - DS * FB * P * 4, DS, FB * P)
        actb, q = place(0, FB, T)
        sg, q = place(q, 2, T)

        xtok2, q = place(0, 5, D)
        gfin, q = place(q, D)
        back, _ = place(q, 10, D)
        htok, _ = place(q, 5, D)
        acte, q = place(q, FB, SLOTS)
        sge, q = place(q, 2, SLOTS)
        yTe, q = place(q, KT, SLOTS)
        yrow, q = place(q, 2, D)
        hTe, q = place(q, KT, SLOTS)
        hrow, q = place(q, 2, D)

        mq1, q = place(0, 2, T)
        after_mq1 = q
        ckvT, q = place(q, 2, T)
        kpeT, q = place(q, T)
        qn, q = place(q, H, T)
        qp, q = place(q, 3, T)
        wuk, q = place(q, 2, H * P)
        assert q - after_mq1 >= 4 * (PSLOTS - 1 - NG) * GP * QHP
        wuv, q = place(q, 2, H * P)
        cktok, q = place(q, 5, KV + ROPE)
        qlat, q = place(q, 2, NB * H)
        qps, q = place(q, NB, 2, H)
        mla0 = q
        cs, q = place(q, 2, T)
        wqn, q = place(q, 3, H * P)
        wqp, q = place(q, 3, H * ROPE)
        raw, q = place(q, 3, T)
        sq1, q = place(q, 3, T)
        rot, q = place(q, T)
        qlr, q = place(q, 3, T)
        knT, q = place(mla0, H, S)
        vtok, q = place(q, NT, H * P)
        Pa, q = place(q, NT, S)
        PTa, q = place(q, NT, S)
        page_slots, q = place(mla0, NG, GP * QHP)
        more_slots, _ = place(after_mq1, PSLOTS - 1 - NG, GP * QHP)
        ckT, _ = place(q, AHEAD + 1, 4 * P)
        wkT, _ = place(q, H, 2 * P)
        q += 4 * (AHEAD + 1) * 4 * P
        kpT, q = place(q, 2, GP // 2 * P)
        Pp2, q = place(q, 2, PAGES * H)
        zrow, q = place(q, ZCOLS)

        def mem_space(at):
            Pm, q = place(at, 2, NT, MEM)
            PTm, q = place(q, 2, 2, S)
            Kb, q = place(q, 2, 2, MEM)
            prod, q = place(q, 2, MEM)
            Vb, q = place(q, NB, 2, MEM)
            return Pm, PTm, Kb, prod, Vb
        mem_bufs = [mem_space(gdn0), mem_space(mla0)]
        mqs = [mq0, mq1]

        bank = [ctx.enter_context(nc.psum_tensor(f"bank{i}", [P, 512], F32))[:, :] for i in range(8)]
        bank_full = [sem(f"bank_full{i}") for i in range(8)]
        bank_free = [sem(f"bank_free{i}") for i in range(8)]
        w_loaded = [sem(f"w_loaded{i}") for i in range(WS)]
        w_used = [sem(f"w_used{i}") for i in range(WS)]
        d_loaded = [sem(f"d_loaded{i}") for i in range(DS)]
        d_used = [sem(f"d_used{i}") for i in range(DS)]

        consts_in = sem("consts_in")
        masks_in = sem("masks_in")
        x_in = sem("x_in")
        rows_in = sem("rows_in")
        conv_in = sem("conv_in")
        mem_in = sem("mem_in")
        small_in = sem("small_in")
        states_in = [sem(f"states_in{i}") for i in range(2)]
        rope_in = sem("rope_in")
        wq_in = sem("wq_in")
        wkv_in = sem("wkv_in")
        zeros = sem("zeros")
        mem_sq = sem("mem_sq")
        mem_scaled = sem("mem_scaled")
        mnT_ready = sem("mnT_ready")
        sq_done = sem("sq_done")
        rstd_ready = sem("rstd_ready")
        h_ready = sem("h_ready")
        upad = sem("upad")
        conv_y = sem("conv_y")
        qkv_ready = sem("qkv_ready")
        cnew_ready = sem("cnew_ready")
        zm_ready = sem("zm_ready")
        gate_in = sem("gate_in")
        gate_ex = sem("gate_ex")
        g_ready = sem("g_ready")
        bg_ready = sem("bg_ready")
        egc_ready = sem("egc_ready")
        l2_sq = sem("l2_sq")
        l2_done = sem("l2_done")
        eg_ready = sem("eg_ready")
        dt_exp = sem("dt_exp")
        qg_ready = sem("qg_ready")
        id_ready = sem("id_ready")
        glx_ready = sem("glx_ready")
        samp_ready = sem("samp_ready")
        qk_prod = sem("qk_prod")
        vs_ready = sem("vs_ready")
        kmask_ready = sem("kmask_ready")
        on_sq = sem("on_sq")
        on_done = sem("on_done")
        ms_max = sem("ms_max")
        ms_norm = sem("ms_norm")
        kb_in = [sem(f"kb_in{i}") for i in range(2)]
        kb_used = sem("kb_used")
        v_in = sem("v_in")
        m32_max = sem("m32_max")
        m32_norm = sem("m32_norm")
        out_done = sem("out_done")
        ck_out = sem("ck_out")
        pd_out = sem("pd_out")
        sd_out = [sem(f"sd_out{i}") for i in range(2)]
        co_out = [sem(f"co_out{i}") for i in range(2)]
        dve_step = sem("dve_step")
        act_step = sem("act_step")
        pool_step = sem("pool_step")
        kv_ready = sem("kv_ready")
        ql_ready = sem("ql_ready")
        qp_ready = sem("qp_ready")
        at_max = sem("at_max")
        at_norm = sem("at_norm")
        own_prod = sem("own_prod")
        pmax_ready = sem("pmax_ready")
        pdiag_ready = sem("pdiag_ready")
        pexp_ready = sem("pexp_ready")
        psum_ready = sem("psum_ready")
        pshift_ready = sem("pshift_ready")
        olat_ready = sem("olat_ready")
        chosen_ready = sem("chosen_ready")
        slot_ready = sem("slot_ready")
        table_ready = sem("table_ready")
        rows_out = sem("rows_out")
        spread = sem("spread")
        hrow_in = sem("hrow_in")
        hx = sem("hx")
        yx = sem("yx")
        back_in = sem("back_in")
        summed = sem("summed")
        normed = sem("normed")
        rooted = sem("rooted")
        out_sq = sem("out_sq")
        gfin_in = sem("gfin_in")
        lg_ready = sem("lg_ready")
        lg_exp = sem("lg_exp")
        mem_out = sem("mem_out")
        half_in = sem("half_in")
        pages_in = [sem(f"pages_in{g}") for g in range(PSLOTS)]
        table_in = sem("table_in")
        page_rows_ready = sem("page_rows_ready")
        groups_used = sem("groups_used")

        def page_slot(G):
            k = G % PSLOTS
            if k < NG:
                v = page_slots[:, k, :]
            elif k < PSLOTS - 1:
                v = more_slots[:, k - NG, :]
            else:
                v = w_ring[:, 5:8].rearrange("p s k c -> p (s k c)")
            return v[:, 0:GP * KV].rearrange("p (g c) -> p g c", g=GP), v[:, GP * KV:GP * QHP]

        result = {}
        uses = [0] * 8
        fulls = [0] * 8
        turn = [0]
        lanes = [8]
        w_uses = [0] * WS
        w_turn = [0]
        w_order = []
        loops = {}

        def claim(pe, key, signal=None, pinned=None):
            b = turn[0] % lanes[0] if pinned is None else pinned
            turn[0] += pinned is None
            n = uses[b]
            uses[b] += 1
            if n:
                pe.wait_ge(bank_free[b], n)
            if signal is None:
                fulls[b] += 1
                signal = bank_full[b], fulls[b]
            result[key] = (b, n) + signal
            return bank[b]

        def full(key):
            return bank_full[result[key][0]]

        def free(key):
            return bank_free[result[key][0]]

        def filled(eng, key):
            b, _, s, v = result[key]
            eng.wait_ge(s, v)
            return bank[b]

        def bank_of(key):
            return bank[result[key][0]]

        def freed(eng, key):
            b, n, _, _ = result[key]
            eng.wait_ge(bank_free[b], n + 1)

        def weights_block(pe, key, rhs, spans):
            s = w_turn[0] % WS
            w_turn[0] += 1
            n = w_uses[s]
            w_uses[s] += 1
            w_order.append((key, s, n))
            pe.wait_ge(w_loaded[s], 16 * (n + 1))
            out = [claim(pe, (key, i), (w_used[s], n + 1)) for i in range(len(spans))]
            for kt in range(KT):
                for i, (lo, hi) in enumerate(spans):
                    mm = pe.matmul(out[i][:, 0:hi - lo], w_ring[:, s, kt, :], rhs[:, kt, lo:hi],
                                   start=(kt == 0), stop=(kt == KT - 1))
            mm.then_inc(w_used[s], 1)

        block = ctx.enter_context(nc.Block())

        @block.tensor
        def _(pe):
            def norm_sum(i, nth, ktiles=KT, src=None):
                src = hT if src is None else src
                pe.wait_ge(sq_done, nth)
                for hf, (lo, hi) in enumerate(HALVES):
                    b = claim(pe, ("ssq", i, hf))
                    for kt in range(ktiles):
                        mm = pe.matmul(b[:, 0:HALF], ones, src[:, kt, lo:hi], start=(kt == 0), stop=(kt == ktiles - 1))
                    mm.then_inc(full(("ssq", i, hf)), 1)

            pe.wait_ge(consts_in, 32)
            pe.wait_ge(rows_in, 80)
            b = claim(pe, "gains")
            for kt in range(KT):
                mm = pe.transpose(b[:, kt * NGAIN:(kt + 1) * NGAIN], gtok[0:NGAIN, kt * P:(kt + 1) * P],
                                  ident[0:NGAIN, 0:NGAIN])
            mm.then_inc(full("gains"), 1)
            pe.wait_ge(mem_scaled, 2)
            for g in range(KT // 2):
                b = claim(pe, ("memT", g))
                for j in range(2):
                    for t in range(2):
                        kt = 2 * g + j
                        mm = pe.transpose(b[:, j * MEM + t * P:j * MEM + (t + 1) * P], mtok[:, t, kt * P:(kt + 1) * P], ident)
                mm.then_inc(full(("memT", g)), 1)
            pe.wait_ge(conv_in, 32)
            b = claim(pe, "convw")
            for j in range(QKV):
                mm = pe.transpose(b[:, j * 28:(j + 1) * 28], cvtok[0:28, j * P:(j + 1) * P], ident[0:28, 0:28])
            mm.then_inc(full("convw"), 1)
            pe.wait_ge(x_in, 80)
            for kt in range(KT):
                b = claim(pe, ("xT", kt))
                for t in range(NT):
                    mm = pe.transpose(b[:, t * P:(t + 1) * P], xtok[:, t, kt * P:(kt + 1) * P], ident)
                mm.then_inc(full(("xT", kt)), 1)
            b = claim(pe, "xTs")
            for kt in range(KT):
                mm = pe.transpose(b[:, kt * NB:(kt + 1) * NB], xtok[0:NB, NT, kt * P:(kt + 1) * P], ident[0:NB, 0:NB])
            mm.then_inc(full("xTs"), 1)

            for l in range(2):
                pe.wait_ge(mnT_ready, KT * (l + 1))
                for blk in range(4):
                    weights_block(pe, ("kv", l, blk), mnT[:, l], [(0, MEM)])
                for t in range(2):
                    b = claim(pe, ("mtok", l, t))
                    for blk in range(4):
                        freed(pe, (("kv", l, blk), 0))
                        mm = pe.transpose(b[:, blk * P:(blk + 1) * P], (memkT if blk < 2 else kvT)[:, l, blk, t * P:(t + 1) * P], ident)
                    mm.then_inc(full(("mtok", l, t)), 1)

            norm_sum(NORM_MIX0, KT)
            pe.wait_ge(h_ready, KT)
            pe.wait_ge(small_in, 112)
            b = claim(pe, "ba")
            for t in range(NT + 1):
                n = P if t < NT else NB
                for kt in range(KT):
                    mm = pe.matmul(b[0:n, t * SEL:(t + 1) * SEL], hT[:, kt, t * P:t * P + n], wba[:, kt, :],
                                   start=(kt == 0), stop=(kt == KT - 1))
            mm.then_inc(full("ba"), 1)
            for blk in range(QKV + H + 2):
                weights_block(pe, ("a", blk), hT, HALVES)
                if blk == 2:
                    pe.wait_ge(g_ready, 1)
                    b = claim(pe, "gcum")
                    pe.matmul(b[:, 0:NT * H], incl, gg[:, 0:NT, :], start=True, stop=True).then_inc(full("gcum"), 1)
                if blk == 4:
                    pe.wait_ge(bg_ready, 1)
                    b = claim(pe, "bgT")
                    for c in range(NT):
                        mm = pe.transpose(b[0:SEL, c * P:(c + 1) * P], BG[:, c, :], ident)
                    mm.then_inc(full("bgT"), 1)
                    b = claim(pe, "bgTs")
                    pe.transpose(b[0:SEL, 0:NB], BG[0:NB, NT, :], ident[0:NB, 0:NB]).then_inc(full("bgTs"), 1)
                if blk == 6:
                    freed(pe, "bgT")
                    freed(pe, "bgTs")
                    b = claim(pe, "bgs")
                    for r in range(SEL):
                        mm = pe.matmul(b[:, r * NB:(r + 1) * NB], sel[:, r, :], BGT[:, S:T], start=True, stop=True)
                    mm.then_inc(full("bgs"), 1)
            pe.wait_ge(cnew_ready, QKV)
            for g in range(5):
                n = min(4, QKV - 4 * g)
                b = claim(pe, ("cn", g))
                for j in range(n):
                    mm = pe.transpose(b[0:11, j * P:(j + 1) * P], cnew[:, 4 * g + j, :], ident)
                mm.then_inc(full(("cn", g)), 1)

            for blk in range(2 * H):
                pe.wait_ge(l2_sq, blk + 1)
                for hf, (lo, hi) in enumerate(HALVES):
                    b = claim(pe, ("l2", blk, hf))
                    pe.matmul(b[:, 0:HALF], ones, sqb[:, blk % 2, lo:hi], start=True, stop=True)\
                      .then_inc(full(("l2", blk, hf)), 1)

            pe.wait_ge(l2_done, 2 * H)
            for grp in range(2):
                heads = [3 * grp + i for i in range(3)]
                for h in heads:
                    b = claim(pe, ("row_b", h))
                    pe.matmul(b, sel[:, h, :], BGT[:, 0:S], start=True, stop=True).then_inc(full(("row_b", h)), 1)
                    b = claim(pe, ("row_g", h))
                    pe.matmul(b, sel[:, H + h, :], BGT[:, 0:S], start=True, stop=True).then_inc(full(("row_g", h)), 1)
                    b = claim(pe, ("kk", h))
                    for c in range(NT):
                        k = qkv[:, H + h, c * P:(c + 1) * P]
                        mm = pe.matmul(b[:, c * P:(c + 1) * P], k, k, start=True, stop=True)
                    mm.then_inc(full(("kk", h)), 1)
                    b = claim(pe, ("qk", h))
                    for c in range(NT):
                        mm = pe.matmul(b[:, c * P:(c + 1) * P], qkv[:, H + h, c * P:(c + 1) * P],
                                       qkv[:, h, c * P:(c + 1) * P], start=True, stop=True)
                    mm.then_inc(full(("qk", h)), 1)
                for lv in range(LEVELS):
                    for i, h in enumerate(heads):
                        if lv == 0:
                            freed(pe, ("kk", h))
                            pe.wait_ge(id_ready, 2 * (h + 1))
                        else:
                            freed(pe, ("Y", h, lv - 1))
                        b = claim(pe, ("X", h, lv))
                        for c in range(NT):
                            mm = pe.matmul(b[:, c * P:(c + 1) * P], LT[:, i, c * P:(c + 1) * P],
                                           Dinv[:, i, c * P:(c + 1) * P], start=True, stop=True)
                        mm.then_inc(full(("X", h, lv)), 1)
                    for i, h in enumerate(heads):
                        freed(pe, ("X", h, lv))
                        if lv:
                            freed(pe, ("Z", h, lv - 1))
                        if lv < LEVELS - 1:
                            b = claim(pe, ("Y", h, lv))
                            for c in range(NT):
                                mm = pe.matmul(b[:, c * P:(c + 1) * P], Einv[:, i, c * P:(c + 1) * P],
                                               Xs[:, i, c * P:(c + 1) * P], start=True, stop=True)
                            mm.then_inc(full(("Y", h, lv)), 1)
                        b = claim(pe, ("Z", h, lv))
                        for c in range(NT):
                            mm = pe.matmul(b[:, c * P:(c + 1) * P], Xs[:, i, c * P:(c + 1) * P],
                                           Einv[:, i, c * P:(c + 1) * P], start=True, stop=True)
                        mm.then_inc(full(("Z", h, lv)), 1)
                for i, h in enumerate(heads):
                    b = claim(pe, ("kt", h))
                    for c in range(NT):
                        mm = pe.transpose(b[:, c * P:(c + 1) * P], qkv[:, H + h, c * P:(c + 1) * P], ident)
                    mm.then_inc(full(("kt", h)), 1)
                    b = claim(pe, ("vt", h))
                    for c in range(NT):
                        mm = pe.transpose(b[:, c * P:(c + 1) * P], qkv[:, 2 * H + h, c * P:(c + 1) * P], ident)
                    mm.then_inc(full(("vt", h)), 1)
                    freed(pe, ("kt", h))
                    freed(pe, ("Z", h, LEVELS - 1))
                    b = claim(pe, ("wT", h))
                    for c in range(NT):
                        mm = pe.matmul(b[:, c * P:(c + 1) * P], kbg[:, c * P:(c + 1) * P],
                                       Einv[:, i, c * P:(c + 1) * P], start=True, stop=True)
                    mm.then_inc(full(("wT", h)), 1)
                for c in range(NT):
                    cc = slice(c * P, (c + 1) * P)
                    for i, h in enumerate(heads):
                        if c == 0:
                            freed(pe, ("vt", h))
                            freed(pe, ("wT", h))
                            freed(pe, ("qk", h))
                            pe.wait_ge(qg_ready, h + 1)
                        else:
                            freed(pe, ("ds", h, c - 1))
                        b = claim(pe, ("vn", h, c))
                        mm = pe.matmul(b[:, 0:P], Einv[:, i, cc], qkv[:, 2 * H + h, cc], start=True, stop=(c == 0))
                        if c:
                            mm = pe.matmul(b[:, 0:P], nWT[:, i, cc], St[:, i, :], start=False, stop=True)
                        mm.then_inc(full(("vn", h, c)), 1)
                    for i, h in enumerate(heads):
                        freed(pe, ("vn", h, c))
                        b = claim(pe, ("o", h, c))
                        mm = pe.matmul(b[:, 0:P], vn[:, i, :], QKT[:, i, cc], start=True, stop=(c == 0))
                        if c:
                            mm = pe.matmul(b[:, 0:P], St[:, i, :], qkv[:, h, cc], start=False, stop=True)
                        mm.then_inc(full(("o", h, c)), 1)
                        b = claim(pe, ("ds", h, c))
                        pe.matmul(b[:, 0:P], qkv[:, H + h, cc], vn[:, i, :], start=True, stop=True)\
                          .then_inc(full(("ds", h, c)), 1)

            for g, n in ((0, 4), (1, 2)):
                b = claim(pe, ("skt", g))
                for j in range(n):
                    mm = pe.transpose(b[0:NB, j * P:(j + 1) * P], qkv[:, H + 4 * g + j, S:T], ident)
                mm.then_inc(full(("skt", g)), 1)
            pe.wait_ge(qk_prod, 1)
            b = claim(pe, "qkd")
            pe.matmul(b[:, 0:H * NB], ones, qkp, start=True, stop=True).then_inc(full("qkd"), 1)
            for h in range(H):
                pe.wait_ge(states_in[h % 2], 16 * (h // 2 + 1))
                b = claim(pe, ("sk", h))
                for n in range(NB):
                    mm = pe.matmul(b[:, 2 * n:2 * n + 2], Ssb[:, h % 2, n * P:(n + 1) * P],
                                   qkv[:, h:h + H + 1:H, S + n], start=True, stop=True)
                mm.then_inc(full(("sk", h)), 1)
                pe.wait_ge(vs_ready, h + 1)
                b = claim(pe, ("vnt", h))
                pe.transpose(b[0:NB, 0:P], vs[:, h, :], ident).then_inc(full(("vnt", h)), 1)
                freed(pe, ("vnt", h))
                pe.wait_ge(kmask_ready, h + 1)
                for half in range(2):
                    b = claim(pe, ("outer", h, half))
                    for j in range(4):
                        n = 4 * half + j
                        mm = pe.matmul(b[:, j * P:(j + 1) * P], kmask[0:NB, n, :], vnt[0:NB, :], start=True, stop=True)
                    mm.then_inc(full(("outer", h, half)), 1)

            for h in range(H):
                pe.wait_ge(on_sq, h + 1)
                for hf, (lo, hi) in enumerate(HALVES):
                    b = claim(pe, ("on", h, hf))
                    pe.matmul(b[:, 0:HALF], ones, sqb[:, h % 2, lo:hi], start=True, stop=True)\
                      .then_inc(full(("on", h, hf)), 1)

            def memory_attention(l):
                Pm, PTm, Kb, prod, Vb = mem_bufs[l]
                mq = mqs[l]

                def scores(m):
                    r = slice((m % 2) * MD, (m % 2) * MD + MD)
                    for j in range(2):
                        b = claim(pe, ("ms", l, m, j))
                        for i in range(2):
                            t = 2 * j + i
                            mm = pe.matmul(b[:, i * MEM:(i + 1) * MEM], mq[r, m // 2, t * P:(t + 1) * P],
                                           memkT[r, l, m // 2, :], start=True, stop=True)
                        mm.then_inc(full(("ms", l, m, j)), 1)

                scores(0)
                for m in range(MH):
                    if m + 1 < MH:
                        scores(m + 1)
                    pe.wait_ge(ms_norm, 8 * l + 2 * (m + 1))
                    for kt in range(2):
                        b = claim(pe, ("mpt", l, m, kt))
                        for t in range(NT):
                            mm = pe.transpose(b[:, t * P:(t + 1) * P], Pm[:, m % 2, t, kt * P:(kt + 1) * P], ident)
                        mm.then_inc(full(("mpt", l, m, kt)), 1)
                    if m % 2 == 1:
                        b = claim(pe, ("mo", l, m // 2))
                        for i in range(2):
                            mh = m - 1 + i
                            for kt in range(2):
                                freed(pe, ("mpt", l, mh, kt))
                                mm = pe.matmul(b[i * MD:(i + 1) * MD, :], memv[:, l, kt, mh * MD:(mh + 1) * MD],
                                               PTm[:, mh % 2, kt, :], start=(kt == 0), stop=(kt == 1))
                        mm.then_inc(full(("mo", l, m // 2)), 1)
                b = claim(pe, ("mqs", l))
                for j in range(2):
                    mm = pe.transpose(b[0:NB, j * P:(j + 1) * P], mq[:, j, S:T], ident)
                mm.then_inc(full(("mqs", l)), 1)
                freed(pe, ("mqs", l))
                for n in range(NB):
                    b = claim(pe, ("mqb", l, n))
                    pe.matmul(b[:, 0:MEM], sel[0:NB, n, :], mqst[0:NB, :], start=True, stop=True)\
                      .then_inc(full(("mqb", l, n)), 1)
                pe.wait_ge(kb_used, NB * (l + 1))
                b = claim(pe, ("mst", l))
                for t in range(2):
                    mm = pe.transpose(b[0:NB * MH, t * P:(t + 1) * P], msc[:, t, :], ident)
                mm.then_inc(full(("mst", l)), 1)
                pe.wait_ge(m32_norm, l + 1)
                b = claim(pe, ("msp", l))
                for t in range(2):
                    mm = pe.transpose(b[:, t * 32:(t + 1) * 32], Pm32[0:32, t * P:(t + 1) * P], ident[0:32, 0:32])
                mm.then_inc(full(("msp", l)), 1)
                freed(pe, ("msp", l))
                pe.wait_ge(v_in, 16 * NB * (l + 1))
                b = claim(pe, ("mos", l))
                for n in range(NB):
                    for j in range(2):
                        for t in range(2):
                            mm = pe.matmul(b[:, (2 * n + j) * 2:(2 * n + j) * 2 + 2], Vb[:, n, t, j * P:(j + 1) * P],
                                           pT[:, t, n * MH + 2 * j:n * MH + 2 * j + 2], start=(t == 0), stop=(t == 1))
                mm.then_inc(full(("mos", l)), 1)

            def mixer_out(l):
                for blk in range(KT):
                    weights_block(pe, ("o", l, blk), hT, HALVES)

            def channel_mixer(name, parts):
                f0, w0, d0 = loops[name] = (list(uses), list(w_uses), [2 * loops["parts"]] * DS)
                assert w_turn[0] % WS == 0
                per = [8] * 4 + [7] * 4
                with pe.Fori(0, parts) as e:
                    for k in range(2 * FB):
                        s, r = k % WS, k // WS
                        pe.wait_ge(w_loaded[s], e * 32 + 16 * (w0[s] + r + 1))
                        for hf in range(2):
                            j = 2 * k + hf
                            pe.wait_ge(bank_free[j % 8], e * per[j % 8] + f0[j % 8] + j // 8)
                        for kt in range(KT):
                            for hf, (lo, hi) in enumerate(HALVES):
                                mm = pe.matmul(bank[(2 * k + hf) % 8][:, 0:HALF], w_ring[:, s, kt, :], hT[:, kt, lo:hi],
                                               start=(kt == 0), stop=(kt == KT - 1))
                        mm.then_inc(w_used[s], 1)
                    for j in range(4 * FB - 6, 4 * FB):
                        if j % 4 >= 2:
                            pe.wait_ge(bank_free[j % 8], e * per[j % 8] + f0[j % 8] + j // 8 + 1)
                    for i in range(KT):
                        s, r = i % DS, i // DS
                        pe.wait_ge(d_loaded[s], e * 32 + 16 * (d0[s] + r + 1))
                        for hf in range(2):
                            j = 4 * FB + 2 * i + hf
                            pe.wait_ge(bank_free[j % 8], e * per[j % 8] + f0[j % 8] + j // 8)
                        for f in range(FB):
                            for hf, (lo, hi) in enumerate(HALVES):
                                mm = pe.matmul(bank[(4 * FB + 2 * i + hf) % 8][:, 0:HALF], d_ring[:, s, f * P:(f + 1) * P],
                                               actb[:, f, lo:hi], start=(f == 0), stop=(f == FB - 1))
                        mm.then_inc(d_used[s], 1)
                for b in range(8):
                    uses[b] += parts * per[b]
                for s in range(WS):
                    w_uses[s] += 2 * parts
                turn[0] = 0
                loops["parts"] += parts

            loops["parts"] = 0
            memory_attention(0)
            pe.wait_ge(on_done, H)
            freed(pe, ("mo", 0, 1))
            pe.wait_ge(samp_ready, 1)
            mixer_out(0)
            norm_sum(NORM_FFN0, 2 * KT)
            pe.wait_ge(h_ready, 2 * KT)
            while w_turn[0] % WS:
                w_turn[0] += 1
            channel_mixer("dense", DENSE_PARTS)

            norm_sum(NORM_KV, 3 * KT)
            pe.wait_ge(h_ready, 3 * KT)
            for blk in range(3):
                weights_block(pe, ("ckv", blk), hT, HALVES)
            pe.wait_ge(h_ready, 4 * KT)
            for blk in range(5):
                weights_block(pe, ("b", blk), hT, HALVES)
            norm_sum("ckv", 3 * KT + 2, 2, sq1)
            freed(pe, (("ckv", 2), 1))
            for hf, (lo, hi) in enumerate(HALVES):
                b = claim(pe, ("kper", hf))
                pe.matmul(b[:, 0:HALF], rotT, raw[:, 2, lo:hi], start=True, stop=True).then_inc(full(("kper", hf)), 1)
            norm_sum("ql", 3 * KT + 5, 3, sq1)
            pe.wait_ge(kv_ready, 1)
            for t in range(NT + 1):
                n = P if t < NT else NB
                b = claim(pe, ("cktok", t))
                for j in range(2):
                    pe.transpose(b[0:n, j * P:(j + 1) * P], ckvT[:, j, t * P:t * P + n], ident)
                pe.transpose(b[0:n, KV:KV + ROPE], kpeT[0:ROPE, t * P:t * P + n], ident[0:ROPE, 0:ROPE])\
                  .then_inc(full(("cktok", t)), 1)
            pe.wait_ge(wq_in, 16 * 6)
            pe.wait_ge(ql_ready, 3)
            for h in range(H):
                for hf, (lo, hi) in enumerate(HALVES):
                    b = claim(pe, ("qn", h, hf))
                    for kt in range(3):
                        mm = pe.matmul(b[:, 0:HALF], wqn[:, kt, h * P:(h + 1) * P], qlr[:, kt, lo:hi],
                                       start=(kt == 0), stop=(kt == 2))
                    mm.then_inc(full(("qn", h, hf)), 1)
            for j in range(3):
                for hf, (lo, hi) in enumerate(HALVES):
                    b = claim(pe, ("qp", j, hf))
                    for kt in range(3):
                        mm = pe.matmul(b[:, 0:HALF], wqp[:, kt, j * P:(j + 1) * P], qlr[:, kt, lo:hi],
                                       start=(kt == 0), stop=(kt == 2))
                    mm.then_inc(full(("qp", j, hf)), 1)
                for hf, (lo, hi) in enumerate(HALVES):
                    freed(pe, ("qp", j, hf))
                    b = claim(pe, ("qpr", j, hf))
                    pe.matmul(b[:, 0:HALF], rotT, sq1[:, j, lo:hi], start=True, stop=True).then_inc(full(("qpr", j, hf)), 1)
            pe.wait_ge(wkv_in, 32)
            pe.wait_ge(qp_ready, 3)
            for h in range(H):
                b = claim(pe, ("kn", h))
                for ct in range(2):
                    mm = pe.matmul(b, wuk[:, ct, h * P:(h + 1) * P], ckvT[:, ct, 0:S], start=(ct == 0), stop=(ct == 1))
                mm.then_inc(full(("kn", h)), 1)
            for t in range(NT):
                for j in range(2):
                    b = claim(pe, ("vtok", t, j))
                    for ct in range(2):
                        mm = pe.matmul(b[:, 0:384], ckvT[:, ct, t * P:(t + 1) * P], wuv[:, ct, j * 384:(j + 1) * 384],
                                       start=(ct == 0), stop=(ct == 1))
                    mm.then_inc(full(("vtok", t, j)), 1)

            def attention_scores(h):
                freed(pe, ("kn", h))
                r = slice((h % 2) * ROPE, (h % 2) * ROPE + ROPE)
                for t in range(NT):
                    n = (t + 1) * P
                    b = claim(pe, ("as", h, t))
                    pe.matmul(b[:, 0:n], qn[:, h, t * P:n], knT[:, h, 0:n], start=True, stop=False)
                    pe.matmul(b[:, 0:n], qp[r, h // 2, t * P:n], kpeT[r, 0:n], start=False, stop=True)\
                      .then_inc(full(("as", h, t)), 1)

            for h in range(H):
                attention_scores(h)
                for kt in range(NT):
                    b = claim(pe, ("apt", h, kt))
                    for t in range(kt, NT):
                        pe.wait_ge(at_norm, NT * h + t + 1)
                        mm = pe.transpose(b[:, t * P:(t + 1) * P], Pa[:, t, kt * P:(kt + 1) * P], ident)
                    mm.then_inc(full(("apt", h, kt)), 1)
                b = claim(pe, ("ao", h))
                for kt in range(NT):
                    freed(pe, ("apt", h, kt))
                    mm = pe.matmul(b[:, kt * P:S], vtok[:, kt, h * P:(h + 1) * P], PTa[:, kt, kt * P:S],
                                   start=(kt == 0), stop=(kt == NT - 1))
                mm.then_inc(full(("ao", h)), 1)
            memory_attention(1)

            for h in range(H):
                b = claim(pe, ("uk", h))
                for ct in range(2):
                    mm = pe.transpose(b[:, ct * P:(ct + 1) * P], wuk[:, ct, h * P:(h + 1) * P], ident)
                mm.then_inc(full(("uk", h)), 1)
            b = claim(pe, "qlat")
            for ct in range(2):
                for h in range(H):
                    freed(pe, ("uk", h))
                    mm = pe.matmul(b[:, (ct * H + h) * NB:(ct * H + h + 1) * NB], wkT[:, h, ct * P:(ct + 1) * P],
                                   qn[:, h, S:T], start=True, stop=True)
            mm.then_inc(full("qlat"), 1)
            b = claim(pe, "qps")
            for j in range(3):
                for odd in range(2):
                    mm = pe.matmul(b[0:ROPE, (2 * j + odd) * NB:(2 * j + odd + 1) * NB], ident[:, odd * ROPE:(odd + 1) * ROPE],
                                   qp[:, j, S:T], start=True, stop=True)
                    mm = pe.matmul(b[ROPE:P, (2 * j + odd) * NB:(2 * j + odd + 1) * NB], ident[:, odd * ROPE:(odd + 1) * ROPE],
                                   qp[:, j, S:T], start=True, stop=True)
            mm.then_inc(full("qps"), 1)
            pe.wait_ge(own_prod, 1)
            b = claim(pe, "own")
            for ct in range(2):
                pe.matmul(b[:, 0:NB * H], ones, ownp[:, ct, :], start=(ct == 0), stop=False)
            pe.matmul(b[:, 0:NB * H], ones[0:ROPE, :], ownp[0:ROPE, 2, :], start=False, stop=True).then_inc(full("own"), 1)

            def turn_pair(k):
                G, j = divmod(k, GP // 2)
                ckv, kpe = page_slot(G)
                if j == 0:
                    pe.wait_ge(pages_in[G % PSLOTS], 16 * 2 * (G // PSLOTS + 1))
                    b = claim(pe, ("kpt", G))
                    for i in range(GP // 2):
                        mm = pe.transpose(b[:, i * P:(i + 1) * P], kpe[:, 2 * i * ROPE:(2 * i + 2) * ROPE], ident)
                    mm.then_inc(full(("kpt", G)), 1)
                b = claim(pe, ("ckt", k))
                for i in range(2):
                    for ct in range(2):
                        mm = pe.transpose(b[:, (2 * i + ct) * P:(2 * i + ct + 1) * P], ckv[:, 2 * j + i, ct * P:(ct + 1) * P], ident)
                mm.then_inc(full(("ckt", k)), 1)

            def summed_values(n):
                freed(pe, ("pv", n))
                b = claim(pe, ("pvT", n))
                for ct in range(2):
                    mm = pe.transpose(b[:, ct * H:(ct + 1) * H], pvs[0:H, ct * P:(ct + 1) * P], ident[0:H, 0:H])
                mm.then_inc(full(("pvT", n)), 1)

            freed(pe, "qlat")
            freed(pe, "qps")
            lanes[0] = 4
            for k in range(AHEAD):
                turn_pair(k)
            for k in range(PAIRS + SP_PAIRS + LAG):
                if k + AHEAD < PAIRS:
                    turn_pair(k + AHEAD)
                before, at = k // SP_PAIRS - 1, k % SP_PAIRS
                if 0 <= before < NB and at == 1:
                    pe.wait_ge(pmax_ready, before + 1)
                    b = claim(pe, ("pmT", before))
                    pe.transpose(b[0:H, 0:P], pmax, ident).then_inc(full(("pmT", before)), 1)
                if 0 <= before < NB and at == 3:
                    pe.wait_ge(pdiag_ready, before + 1)
                    b = claim(pe, ("pmB", before))
                    pe.matmul(b[:, 0:H], ones[0:H, :], pdiag[0:H, :], start=True, stop=True).then_inc(full(("pmB", before)), 1)
                v = k - SP_PAIRS - LAG
                if 0 <= v:
                    sample, vpair = divmod(v, SP_PAIRS)
                    vG, vj = divmod(v, GP // 2)
                    values, _ = page_slot(vG)
                    if vpair == 0:
                        pe.wait_ge(pexp_ready, 2 * (sample + 1))
                        pv = claim(pe, ("pv", sample), (groups_used, NG * (sample + 1)), pinned=4 + sample % 2)

                def value_product(i, ct):
                    if v >= 0:
                        mm = pe.matmul(pv[0:H, ct * P:(ct + 1) * P], Pp2[:, sample % 2, (2 * vpair + i) * H:(2 * vpair + i + 1) * H],
                                       values[:, 2 * vj + i, ct * P:(ct + 1) * P], start=(vpair == 0 and i == 0 and ct == 0),
                                       stop=(vpair == SP_PAIRS - 1 and i == 1), skip_group_check=True)
                        if i and ct and vj == GP // 2 - 1:
                            mm.then_inc(groups_used, 1)

                if k < PAIRS:
                    n, pair = divmod(k, SP_PAIRS)
                    G, j = divmod(k, GP // 2)
                    if pair == 0:
                        sc = claim(pe, ("sc", n), pinned=6 + n % 2)
                    freed(pe, ("ckt", k))
                    freed(pe, ("kpt", G))
                    cols = 2 * pair * H
                    pe.matmul(sc[:, cols:cols + 2 * H], kpT[:, G % 2, j * P:(j + 1) * P], qps[:, n].rearrange("p a h -> p (a h)"),
                              start=True, stop=False, skip_group_check=True)
                for i in range(2):
                    for ct in range(2):
                        value_product(i, ct)
                        if k < PAIRS:
                            mm = pe.matmul(sc[:, cols + i * H:cols + (i + 1) * H], ckT[:, k % (AHEAD + 1), (2 * i + ct) * P:(2 * i + ct + 1) * P],
                                           qlat[:, ct, n * H:(n + 1) * H], start=False, stop=(ct == 1), skip_group_check=True)
                if k < PAIRS and pair == SP_PAIRS - 1:
                    mm.then_inc(full(("sc", n)), 1)
                if v >= 0:
                    n, pair = sample, vpair
                    if pair == 1:
                        pe.wait_ge(psum_ready, n + 1)
                        b = claim(pe, ("ptot", n))
                        pe.matmul(b[:, 0:H], ones, psums, start=True, stop=True).then_inc(full(("ptot", n)), 1)
                    if pair == 2 and n:
                        summed_values(n - 1)
            summed_values(NB - 1)
            lanes[0] = 8
            pe.wait_ge(olat_ready, NB)
            b = claim(pe, "ov")
            for h in range(H):
                for ct in range(2):
                    mm = pe.matmul(b[:, h * NB:(h + 1) * NB], wuv[:, ct, h * P:(h + 1) * P], olat[:, ct, h * NB:(h + 1) * NB],
                                   start=(ct == 0), stop=(ct == 1))
            mm.then_inc(full("ov"), 1)
            freed(pe, "ov")
            freed(pe, ("ao", H - 1))
            freed(pe, ("mo", 1, 1))
            pe.wait_ge(samp_ready, 2)
            mixer_out(1)

            norm_sum(NORM_FFN1, 4 * KT + 5)
            pe.wait_ge(h_ready, 5 * KT)
            b = claim(pe, "rt")
            for t in range(NT + 1):
                n = P if t < NT else NB
                for kt in range(KT):
                    mm = pe.matmul(b[0:n, t * NE:(t + 1) * NE], hT[:, kt, t * P:t * P + n], wrt[:, kt, :],
                                   start=(kt == 0), stop=(kt == KT - 1))
            mm.then_inc(full("rt"), 1)
            for name, src in (("ht", hT), ("xt", xT)):
                for t in range(NT + 1):
                    n = P if t < NT else NB
                    for j in range(2):
                        b = claim(pe, (name, t, j))
                        for i in range(4):
                            mm = pe.transpose(b[0:n, i * P:(i + 1) * P], src[:, 4 * j + i, t * P:t * P + n], ident)
                        mm.then_inc(full((name, t, j)), 1)
                if name == "ht":
                    pe.wait_ge(chosen_ready, 1)
                    b = claim(pe, "upto")
                    for t in range(NT + 2):
                        for u in range(min(t + 1, NT + 1)):
                            n = P if u < NT else NB
                            mm = pe.matmul(b[:, t * NE:(t + 1) * NE], (incl if u == t else ones)[0:n, :], chosen[0:n, u, :],
                                           start=(u == 0), stop=(u == min(t, NT)))
                    mm.then_inc(full("upto"), 1)

            def expert_tokens(g, b):
                for j in range(2):
                    for r in range(2):
                        mm = pe.transpose(b[:, j * SLOTS + r * ROWS:j * SLOTS + (r + 1) * ROWS],
                                          hrow[0:ROWS, r, (2 * g + j) * P:(2 * g + j + 1) * P], ident[0:ROWS, 0:ROWS])
                mm.then_inc(hx, 1)

            pe.wait_ge(hrow_in, 16)
            for g in range(4):
                expert_tokens(g, claim(pe, ("hx", g), (hx, g + 1), pinned=6 + g % 2))
            pe.wait_ge(bank_free[6], uses[6])
            pe.wait_ge(bank_free[7], uses[7])
            while w_turn[0] % WS:
                w_turn[0] += 1
            f0, w0, d0 = loops["experts"] = (list(uses), list(w_uses), [2 * loops["parts"]] * DS)
            per = EXPERT_USES
            pe.wait_ge(table_ready, 1)
            n_passes = pe.value_load(table[0:1, PASSES:PASSES + 1], min_val=1, max_val=PASSES)
            with pe.Fori(0, PASSES) as p:
                with pe.If(p < n_passes):
                    for k in range(2 * FB):
                        s, r = k % WS, k // WS
                        f, bk = k // 2, 2 * (k % 2) + k // 2 % 2
                        pe.wait_ge(w_loaded[s], p * 32 + 16 * (w0[s] + r + 1))
                        pe.wait_ge(bank_free[bk], p * per[bk] + f0[bk] + f // 2)
                        for kt in range(KT):
                            mm = pe.matmul(bank[bk][:, 0:SLOTS], w_ring[:, s, kt, :], hTe[:, kt, :],
                                           start=(kt == 0), stop=(kt == KT - 1))
                        mm.then_inc(w_used[s], 1)
                    pe.wait_ge(hrow_in, p * 16 + 32)
                    for g in range(4):
                        bk = 6 + g % 2
                        pe.wait_ge(bank_free[bk], p * per[bk] + f0[bk] + g // 2)
                        expert_tokens(g, bank[bk])
                    for bk in (2, 3):
                        pe.wait_ge(bank_free[bk], p * per[bk] + f0[bk] + per[bk])

                    def results(i):
                        bk = 6 + i % 2
                        pe.wait_ge(bank_free[4 + i % 2], p * 4 + f0[4 + i % 2] + i // 2 + 1)
                        pe.wait_ge(bank_free[bk], p * per[bk] + f0[bk] + 2 + i // 2)
                        for r in range(2):
                            mm = pe.transpose(bank[bk][0:ROWS, r * P:(r + 1) * P], yTe[:, i, r * ROWS:(r + 1) * ROWS], ident)
                        mm.then_inc(yx, 1)

                    for i in range(KT):
                        s, r = i % DS, i // DS
                        bk = 4 + i % 2
                        pe.wait_ge(d_loaded[s], p * 32 + 16 * (d0[s] + r + 1))
                        pe.wait_ge(bank_free[bk], p * 4 + f0[bk] + i // 2)
                        for f in range(FB):
                            mm = pe.matmul(bank[bk][:, 0:SLOTS], d_ring[:, s, f * P:(f + 1) * P], acte[:, f, :],
                                           start=(f == 0), stop=(f == FB - 1))
                        mm.then_inc(d_used[s], 1)
                        if i:
                            results(i - 1)
                    results(KT - 1)

        @block.vector
        def _(dve):
            steps = [0]

            def link(ins):
                steps[0] += 1
                ins.then_inc(dve_step, 1)
                dve.wait_ge(dve_step, steps[0])

            def norm(i, g, nth, new=True):
                if new:
                    freed(dve, ("ssq", i, 1))
                    link(dve.reciprocal(rstd, rstd))
                for kt in range(KT):
                    dve.scalar_tensor_tensor(out=hT[:, kt, :], in0=xT[:, kt, :], scalar=gains[:, kt, GAIN[g]:GAIN[g] + 1],
                                             in1=rstd, op0=ALU.mult, op1=ALU.mult).then_inc(h_ready, 1)

            dve.wait_ge(mem_sq, 3)
            link(dve.reciprocal(memss, memss))
            for t in range(2):
                dve.tensor_scalar(mtok[:, t, :], mtok[:, t, :], memss[:, t:t + 1], None, ALU.mult).then_inc(mem_scaled, 1)
            filled(dve, "gains")
            dve.tensor_copy(gains.rearrange("p a b -> p (a b)"), bank_of("gains")[:, 0:KT * NGAIN]).then_inc(free("gains"), 1)
            freed(dve, "gains")
            for l in range(2):
                for kt in range(KT):
                    b = filled(dve, ("memT", kt // 2))
                    dve.tensor_scalar(mnT[:, l, kt, :], b[:, (kt % 2) * MEM:(kt % 2 + 1) * MEM],
                                      gains[:, kt, GAIN_MEM + l:GAIN_MEM + l + 1], None, ALU.mult).then_inc(mnT_ready, 1)
            dve.wait_ge(mnT_ready, 2 * KT)
            for g in range(KT // 2):
                dve.engine_nop().then_inc(free(("memT", g)), 1)
            dve.wait_ge(table_in, 16 * GP)
            dve.tensor_copy(page_f, page_rows).then_inc(page_rows_ready, 1)
            dve.wait_ge(page_rows_ready, 1)
            link(dve.tensor_scalar(page_f, page_f, float(P // GP), run, ALU.mult, ALU.add))
            dve.tensor_copy(page_rows, page_f).then_inc(page_rows_ready, 1)
            b = filled(dve, "convw")
            dve.tensor_copy(convw.rearrange("p a b -> p (a b)"), b[:, 0:QKV * 28]).then_inc(free("convw"), 1)
            for kt in range(KT):
                b = filled(dve, ("xT", kt))
                dve.tensor_copy(xT[:, kt, 0:S], b).then_inc(free(("xT", kt)), 1)
            b = filled(dve, "xTs")
            dve.tensor_copy(xT[:, :, S:T], b[:, 0:KT * NB].rearrange("p (k n) -> p k n", k=KT)).then_inc(free("xTs"), 1)
            freed(dve, "xTs")
            freed(dve, "convw")
            norm(NORM_MIX0, NORM_MIX0, 1)

            def gate_inputs():
                b = filled(dve, "ba")
                dve.wait_ge(zeros, 3)
                dve.tensor_copy(GB[:, 0:NT, :], b[:, 0:NT * SEL].rearrange("p (a b) -> p a b", a=NT))
                link(dve.tensor_copy(GB[0:NB, NT, :], b[0:NB, NT * SEL:(NT + 1) * SEL]))
                dve.engine_nop().then_inc(free("ba"), 1)
                dve.wait_ge(small_in, 112)
                link(dve.tensor_tensor(A1, GB[:, :, H:SEL], dtb.unsqueeze(1).to_broadcast([P, 5, H]), ALU.add))
                dve.scalar_tensor_tensor(out=AB, in0=A1, scalar=-1.0, in1=A1, op0=ALU.mult, op1=ALU.max).then_inc(gate_in, 1)

            def gate_values():
                dve.wait_ge(gate_ex, 4)
                link(dve.scalar_tensor_tensor(out=A1, in0=A1, scalar=0.0, in1=E1, op0=ALU.max, op1=ALU.add))
                link(dve.tensor_scalar(EB, EB, 1.0, None, ALU.add))
                dve.scalar_tensor_tensor(out=gg, in0=A1, scalar=-1.0, in1=EA.unsqueeze(1).to_broadcast([P, 5, H]),
                                         op0=ALU.mult, op1=ALU.mult).then_inc(g_ready, 1)
                dve.wait_ge(g_ready, 1)
                link(dve.reciprocal(BG[:, :, 0:H], EB))
                link(dve.tensor_copy(BG[0:NB, NT, H:SEL], gg[0:NB, NT, :]))

            def gate_sums():
                b = filled(dve, "gcum")
                dve.tensor_copy(BG[:, 0:NT, H:SEL], b[:, 0:NT * H].rearrange("p (a b) -> p a b", a=NT)).then_inc(free("gcum"), 1)
                freed(dve, "gcum")
                dve.engine_nop().then_inc(bg_ready, 1)

            def gate_rows():
                filled(dve, "bgT")
                dve.tensor_copy(BGT[:, 0:S], bank_of("bgT")[0:SEL, :]).then_inc(free("bgT"), 1)
                filled(dve, "bgTs")
                dve.tensor_copy(BGT[:, S:T], bank_of("bgTs")[0:SEL, 0:NB]).then_inc(free("bgTs"), 1)
                dve.wait_ge(egc_ready, 1)
                link(dve.tensor_tensor(begc, BG[:, 0:NT, 0:H], egc, ALU.mult))

            gate_inputs()
            for blk in range(QKV):
                u, y = U[:, blk % 2, :], Y[:, blk % 2, :]
                freed(dve, (("a", blk), 1))
                freed(dve, (("a", blk), 0))
                dve.wait_ge(upad, 2 + blk + 1)
                if blk >= 2:
                    dve.wait_ge(qkv_ready, 2 * (blk - 1))
                for j in range(CW):
                    tap = convw[:, blk, 24 + j:25 + j]
                    if j == 0:
                        dve.tensor_scalar(y, u[:, 0:CONVW], tap, None, ALU.mult).then_inc(conv_y, 1)
                    else:
                        dve.wait_ge(conv_y, CW * blk + j)
                        dve.scalar_tensor_tensor(out=y, in0=u[:, j:j + CONVW], scalar=tap, in1=y, op0=ALU.mult,
                                                 op1=ALU.add).then_inc(conv_y, 1)
                if blk == 0:
                    gate_values()
                if blk == 3:
                    gate_sums()
                if blk == 5:
                    gate_rows()

            for blk in range(2 * H):
                freed(dve, ("l2", blk, 1))
                link(dve.reciprocal(nrb[:, blk % 2, :], nrb[:, blk % 2, :]))
                dve.tensor_tensor(qkv[:, blk, :], qkv[:, blk, :], nrb[:, blk % 2, :], ALU.mult).then_inc(l2_done, 1)
            dve.wait_ge(l2_done, 2 * H)
            dve.tensor_tensor(qkp, qkv[:, 0:H, S:T], qkv[:, H:2 * H, S:T], ALU.mult).then_inc(qk_prod, 1)

            bc4 = [P, NT, P]
            dve.wait_ge(mem_out, 128)
            for grp in range(2):
                heads = [3 * grp + i for i in range(3)]
                for i, h in enumerate(heads):
                    dve.wait_ge(eg_ready, h + 1)
                    b = filled(dve, ("row_g", h))
                    for c in range(NT):
                        dve.tensor_scalar(DT[:, c * P:(c + 1) * P], b[:, c * P:(c + 1) * P], BG[:, c, H + h:H + h + 1], 0.0,
                                          ALU.subtract, ALU.min)
                    dve.tensor_tensor(kgt, b[:, P - 1:S:P], BG[:, 0:NT, H + h], ALU.subtract).then_inc(free(("row_g", h)), 1)
                    dve.tensor_copy(glx[:, h, :], EG[:, P - 1:S:P]).then_inc(glx_ready, 1)
                    dve.wait_ge(dt_exp, 2 * h + 2)
                    b = filled(dve, ("row_b", h))
                    if h == 3:
                        filled(dve, ("wT", 2))
                    link(dve.scalar_tensor_tensor(out=t1, in0=b, scalar=-1.0, in1=DT, op0=ALU.mult, op1=ALU.mult))
                    dve.engine_nop().then_inc(free(("row_b", h)), 1)
                    b = filled(dve, ("kk", h))
                    dve.tensor_tensor(LT[:, i, :], b, t1, ALU.mult).then_inc(free(("kk", h)), 1)
                    freed(dve, ("kk", h))
                    link(dve.tensor_tensor(DT.rearrange("p (c i) -> p c i", c=NT), DT.rearrange("p (c i) -> p c i", c=NT),
                                           incl.unsqueeze(1).to_broadcast(bc4), ALU.mult))
                    b = filled(dve, ("qk", h))
                    dve.tensor_tensor(QKT[:, i, :], b, DT, ALU.mult).then_inc(free(("qk", h)), 1)
                    freed(dve, ("qk", h))
                dve.wait_ge(masks_in, 16)
                dve.wait_ge(id_ready, 2 * (3 * grp + 3))
                for lv in range(LEVELS):
                    for i, h in enumerate(heads):
                        def pick(key, dst, m):
                            b = filled(dve, key)
                            dve.copy_predicated(out=dst.rearrange("p (c i) -> p c i", c=NT),
                                                mask=lmask[:, m, :].unsqueeze(1).to_broadcast(bc4),
                                                data=b.rearrange("p (c i) -> p c i", c=NT)).then_inc(free(key), 1)
                        if lv < LEVELS - 1:
                            pick(("Y", h, lv), Dinv[:, i, :], lv)
                        pick(("Z", h, lv), Einv[:, i, :], LEVELS + lv)
                for i, h in enumerate(heads):
                    b = filled(dve, ("kt", h))
                    if i:
                        filled(dve, ("wT", h - 1))
                    for c in range(NT):
                        cc = slice(c * P, (c + 1) * P)
                        dve.tensor_scalar(kbg[:, cc], b[:, cc], begc[:, c, h:h + 1], None, ALU.mult)
                    for c in range(NT):
                        cc = slice(c * P, (c + 1) * P)
                        ins = dve.tensor_scalar(qkv[:, H + h, cc], b[:, cc], kgs[:, h, c:c + 1], None, ALU.mult)
                    ins.then_inc(free(("kt", h)), 1)
                for c in range(NT):
                    cc = slice(c * P, (c + 1) * P)
                    for i, h in enumerate(heads):
                        b = filled(dve, ("o", h, c))
                        dve.tensor_copy(hT[:, h, cc], b[:, 0:P]).then_inc(free(("o", h, c)), 1)
                        b = filled(dve, ("ds", h, c))
                        if c == 0:
                            if grp == 1 and i == 0:
                                dve.wait_ge(pd_out, 48)
                            dve.tensor_copy(St[:, i, :], b[:, 0:P]).then_inc(free(("ds", h, c)), 1)
                        else:
                            freed(dve, ("ds", h, c - 1))
                            dve.scalar_tensor_tensor(out=St[:, i, :], in0=St[:, i, :], scalar=glx[:, h, c:c + 1], in1=b[:, 0:P],
                                                     op0=ALU.mult, op1=ALU.add).then_inc(free(("ds", h, c)), 1)

            b = filled(dve, "qkd")
            dve.tensor_copy(qkd.rearrange("p a b -> p (a b)"), b[:, 0:H * NB]).then_inc(free("qkd"), 1)
            freed(dve, "qkd")
            for h in range(H):
                b = filled(dve, ("sk", h))
                link(dve.tensor_tensor(sa, b[:, 1:2 * NB:2], egs[:, h, :], ALU.mult))
                link(dve.tensor_tensor(sa, qkv[:, 2 * H + h, S:T], sa, ALU.subtract))
                dve.tensor_tensor(vs[:, h, :], sa, bsamp[:, h, :], ALU.mult).then_inc(vs_ready, 1)
                dve.tensor_tensor(sbb, b[:, 0:2 * NB:2], egs[:, h, :], ALU.mult).then_inc(free(("sk", h)), 1)
                dve.wait_ge(vs_ready, h + 1)
                link(dve.tensor_tensor(sa, vs[:, h, :], qkd[:, h, :], ALU.mult))
                freed(dve, ("sk", h))
                link(dve.tensor_tensor(hT[:, h, S:T], sa, sbb, ALU.add))
                for half in range(2):
                    b = filled(dve, ("outer", h, half))
                    for j in range(4):
                        n = 4 * half + j
                        st = Ssb[:, h % 2, n * P:(n + 1) * P]
                        ins = dve.scalar_tensor_tensor(out=st, in0=st, scalar=egs[:, h, n:n + 1], in1=b[:, j * P:(j + 1) * P],
                                                       op0=ALU.mult, op1=ALU.add)
                    ins.then_inc(free(("outer", h, half)), 1)

            dve.wait_ge(small_in, 112)
            for h in range(H):
                freed(dve, ("on", h, 1))
                link(dve.reciprocal(nrb[:, h % 2, :], nrb[:, h % 2, :]))
                link(dve.scalar_tensor_tensor(out=hT[:, h, :], in0=hT[:, h, :], scalar=g_on[:, 0:1], in1=nrb[:, h % 2, :],
                                              op0=ALU.mult, op1=ALU.mult))
                dve.tensor_tensor(hT[:, h, :], hT[:, h, :], zs[:, h, :], ALU.mult).then_inc(on_done, 1)

            def memory_attention(l):
                Pm, PTm, Kb, prod, Vb = mem_bufs[l]
                for m in range(MH):
                    for j in range(2):
                        key = ("ms", l, m, j)
                        b = filled(dve, key)
                        link(dve.tensor_reduce(mmax[:, m, j, :], b.rearrange("p (a k) -> p a k", a=2), X, ALU.max, negate=True))
                        dve.tensor_scalar(mmax[:, m, j, :], mmax[:, m, j, :], MEM_SCALE, None, ALU.mult).then_inc(ms_max, 1)
                    for j in range(2):
                        key = ("ms", l, m, j)
                        freed(dve, key)
                        link(dve.reciprocal(msum[:, m, j, :], msum[:, m, j, :]))
                        for i in range(2):
                            t = 2 * j + i
                            ins = dve.tensor_scalar(Pm[:, m % 2, t, :], Pm[:, m % 2, t, :], msum[:, m, j, i:i + 1], None, ALU.mult)
                        ins.then_inc(ms_norm, 1)
                for n in range(NB):
                    dve.wait_ge(kb_in[n % 2], 16 * (NB // 2 * l + n // 2 + 1))
                    b = filled(dve, ("mqb", l, n))
                    dve.tensor_tensor(prod, Kb[:, n % 2], b[:, 0:MEM].unsqueeze(1).to_broadcast([P, 2, MEM]), ALU.mult)\
                       .then_inc(free(("mqb", l, n)), 1)
                    freed(dve, ("mqb", l, n))
                    dve.tensor_reduce(msc[:, :, n * MH:(n + 1) * MH], prod.rearrange("p t (h d) -> p t h d", h=MH), X, ALU.add)\
                       .then_inc(kb_used, 1)
                    dve.wait_ge(kb_used, NB * l + n + 1)
                key = ("mst", l)
                b = filled(dve, key)
                link(dve.tensor_reduce(m32[0:32, :], b[0:32, 0:MEM], X, ALU.max, negate=True))
                dve.tensor_scalar(m32[0:32, :], m32[0:32, :], MEM_SCALE, None, ALU.mult).then_inc(m32_max, 1)
                freed(dve, key)
                link(dve.reciprocal(s32[0:32, :], s32[0:32, :]))
                dve.tensor_scalar(Pm32[0:32, :], Pm32[0:32, :], s32[0:32, :], None, ALU.mult).then_inc(m32_norm, 1)
                key = ("mos", l)
                b = filled(dve, key)
                for odd in range(2):
                    r = slice(odd * MD, odd * MD + MD)
                    v = b[r, 0:4 * NB].rearrange("p (n j c) -> p j n c", n=NB, j=2)
                    for j in range(2):
                        ins = dve.tensor_copy(hT[r, H + j, S:T], v[:, j, :, odd])
                ins.then_inc(free(key), 1)
                freed(dve, key)
                dve.engine_nop().then_inc(samp_ready, 1)

            def add_to_stream(key, blk, hf):
                b = filled(dve, key)
                lo, hi = HALVES[hf]
                dve.tensor_tensor(xT[:, blk, lo:hi], xT[:, blk, lo:hi], b[:, 0:HALF], ALU.add).then_inc(free(key), 1)

            def channel_mixer(name, parts):
                f0, w0, d0 = loops[name]
                per = [8] * 4 + [7] * 4
                with dve.Fori(0, parts) as e:
                    dve.wait_ge(d_used[DS - 1], e * 2 + d0[DS - 1])
                    for f in range(FB):
                        k = 2 * f + 1
                        for hf, (lo, hi) in enumerate(HALVES):
                            ju, jg = 4 * f + 2 + hf, 4 * f + hf
                            dve.wait_ge(w_used[k % WS], e * 2 + w0[k % WS] + k // WS + 1)
                            dve.wait_ge(bank_free[jg % 8], e * per[jg % 8] + f0[jg % 8] + jg // 8 + 1)
                            dve.tensor_tensor(actb[:, f, lo:hi], sg[:, f % 2, lo:hi], bank[ju % 8][:, 0:HALF], ALU.mult)\
                               .then_inc(bank_free[ju % 8], 1)
                    for i in range(KT):
                        for hf, (lo, hi) in enumerate(HALVES):
                            j = 4 * FB + 2 * i + hf
                            dve.wait_ge(d_used[i % DS], e * 2 + d0[i % DS] + i // DS + 1)
                            dve.tensor_tensor(xT[:, i, lo:hi], xT[:, i, lo:hi], bank[j % 8][:, 0:HALF], ALU.add)\
                               .then_inc(bank_free[j % 8], 1)
                for b in range(4, 8):
                    dve.wait_ge(bank_free[b], parts * per[b] + f0[b])
                for b in range(4):
                    dve.wait_ge(bank_free[b], parts * per[b] + f0[b])

            memory_attention(0)
            for blk in range(KT):
                for hf in range(2):
                    add_to_stream((("o", 0, blk), hf), blk, hf)
            for blk in range(KT):
                freed(dve, (("o", 0, blk), 1))
            norm(NORM_FFN0, NORM_FFN0, 2)
            channel_mixer("dense", DENSE_PARTS)

            norm(NORM_KV, NORM_KV, 3)
            filled(dve, (("ckv", 2), 1))
            norm(NORM_MIX1, NORM_MIX1, 3, new=False)
            freed(dve, ("ssq", "ckv", 1))
            link(dve.reciprocal(rstd, rstd))
            for j in range(2):
                dve.scalar_tensor_tensor(out=ckvT[:, j, :], in0=raw[:, j, :], scalar=g_ck[:, j:j + 1], in1=rstd,
                                         op0=ALU.mult, op1=ALU.mult)
            dve.wait_ge(rope_in, 16)

            def rotate(dst, src, keys, signal):
                for hf, (lo, hi) in enumerate(HALVES):
                    b = filled(dve, keys[hf])
                    dve.tensor_tensor(rot[:, lo:hi], b[:, 0:HALF], cs[:, 1, lo:hi], ALU.mult).then_inc(free(keys[hf]), 1)
                link(dve.tensor_tensor(dst, src, cs[:, 0, :], ALU.mult))
                freed(dve, keys[1])
                freed(dve, keys[0])
                dve.tensor_tensor(dst, dst, rot, ALU.add).then_inc(signal, 1)

            rotate(kpeT, raw[:, 2, :], [("kper", 0), ("kper", 1)], kv_ready)
            dve.wait_ge(kv_ready, 1)
            freed(dve, ("ssq", "ql", 1))
            link(dve.reciprocal(rstd, rstd))
            for j in range(3):
                dve.scalar_tensor_tensor(out=qlr[:, j, :], in0=qlr[:, j, :], scalar=g_ql[:, j:j + 1], in1=rstd,
                                         op0=ALU.mult, op1=ALU.mult).then_inc(ql_ready, 1)
            for t in range(NT + 1):
                n = P if t < NT else NB
                b = filled(dve, ("cktok", t))
                dve.tensor_copy(cktok[0:n, t, :], b[0:n, 0:KV + ROPE]).then_inc(free(("cktok", t)), 1)
            for j in range(3):
                rotate(qp[:, j, :], sq1[:, j, :], [("qpr", j, 0), ("qpr", j, 1)], qp_ready)
                dve.wait_ge(qp_ready, j + 1)
            for t in range(NT):
                for j in range(2):
                    b = filled(dve, ("vtok", t, j))
                    dve.tensor_copy(vtok[:, t, j * 384:(j + 1) * 384], b[:, 0:384]).then_inc(free(("vtok", t, j)), 1)
            for h in range(H):
                for t in range(NT):
                    n = (t + 1) * P
                    b = filled(dve, ("as", h, t))
                    link(dve.tensor_tensor(b[:, t * P:n], b[:, t * P:n], cmask, ALU.add))
                    link(dve.tensor_reduce(atmax[:, h, t:t + 1], b[:, 0:n], X, ALU.max, negate=True))
                    dve.tensor_scalar(atmax[:, h, t:t + 1], atmax[:, h, t:t + 1], MLA_SCALE, None, ALU.mult).then_inc(at_max, 1)
                for t in range(NT):
                    n = (t + 1) * P
                    freed(dve, ("as", h, t))
                    link(dve.reciprocal(atsum[:, h, t:t + 1], atsum[:, h, t:t + 1]))
                    dve.tensor_scalar(Pa[:, t, 0:n], Pa[:, t, 0:n], atsum[:, h, t:t + 1], None, ALU.mult).then_inc(at_norm, 1)
            memory_attention(1)

            b = filled(dve, "qlat")
            dve.tensor_copy(qlat.rearrange("p c (n h) -> p c h n", n=NB),
                            b[:, 0:2 * H * NB].rearrange("p (c h n) -> p c h n", c=2, h=H)).then_inc(free("qlat"), 1)
            b = filled(dve, "qps")
            dve.wait_ge(zeros, 4)
            for i in range(2):
                r = slice(i * ROPE, (i + 1) * ROPE)
                ins = dve.tensor_copy(qps[r, :, i, :].rearrange("p n h -> p h n"), b[r, 0:H * NB].rearrange("p (h n) -> p h n", h=H))
            ins.then_inc(free("qps"), 1)
            freed(dve, "qlat")
            freed(dve, "qps")
            for ct in range(2):
                dve.tensor_tensor(ownp[:, ct, :].rearrange("p (n h) -> p n h", n=NB), qlat[:, ct, :].rearrange("p (n h) -> p n h", n=NB),
                                  ckvT[:, ct, S:T].unsqueeze(2).to_broadcast([P, NB, H]), ALU.mult)
            dve.tensor_tensor(ownp[0:ROPE, 2, :].rearrange("p (n h) -> p n h", n=NB), qps[0:ROPE, :, 0, :],
                              kpeT[0:ROPE, S:T].unsqueeze(2).to_broadcast([ROPE, NB, H]), ALU.mult).then_inc(own_prod, 1)
            b = filled(dve, "own")
            dve.tensor_copy(own, b[:, 0:NB * H]).then_inc(free("own"), 1)
            freed(dve, "own")
            dve.tensor_copy(ownv, ckvT[:, :, S:T]).then_inc(own_prod, 1)

            def turned(k):
                if k % 2 == 0:
                    b = filled(dve, ("ckt", k))
                    dve.tensor_copy(ckT[:, k % (AHEAD + 1), :], b).then_inc(free(("ckt", k)), 1)

            for k in range(AHEAD):
                turned(k)
            for k in range(PAIRS + SP_PAIRS + LAG + 4):
                if k + AHEAD < PAIRS:
                    turned(k + AHEAD)
                n, at = k // SP_PAIRS - 1, k % SP_PAIRS
                if 0 <= n < NB:
                    mine = own[:, n * H:(n + 1) * H]
                    exn, tot, Pp = exn2[:, n % 2, :], tot2[:, n % 2, :], Pp2[:, n % 2, :]
                    if at == 0:
                        b = filled(dve, ("sc", n))
                        dve.tensor_reduce(pmax, b[:, 0:PAGES * H].rearrange("p (g h) -> p h g", h=H), X, ALU.max).then_inc(pmax_ready, 1)
                    if at == 1:
                        bt = filled(dve, ("pmT", n))
                        dve.tensor_reduce(pmx[0:H, :], bt[0:H, 0:P], X, ALU.max).then_inc(free(("pmT", n)), 1)
                        freed(dve, ("pmT", n))
                        dve.tensor_scalar(pdiag[0:H, :], ident[0:H, 0:H], pmx[0:H, :], None, ALU.mult).then_inc(pdiag_ready, 1)
                    if at == 3:
                        bm = filled(dve, ("pmB", n))
                        dve.tensor_tensor(mxb, bm[:, 0:H], mine, ALU.max).then_inc(free(("pmB", n)), 1)
                        freed(dve, ("pmB", n))
                        if n > 1:
                            filled(dve, ("pv", n - 2))
                        dve.tensor_tensor(exn, mine, mxb, ALU.subtract)
                        pages = bank_of(("sc", n))[:, 0:PAGES * H].rearrange("p (g h) -> p g h", h=H)
                        dve.tensor_tensor(Pp.rearrange("p (g h) -> p g h", h=H), pages, mxb.unsqueeze(1).to_broadcast([P, PAGES, H]),
                                          ALU.subtract).then_inc(free(("sc", n)), 1)
                    if at == 5:
                        dve.wait_ge(pexp_ready, 2 * n + 2)
                        if n:
                            filled(dve, ("ptot", n - 1))
                        dve.tensor_reduce(psums, Pp.rearrange("p (g h) -> p h g", h=H), X, ALU.add).then_inc(psum_ready, 1)
                    if at == LAG + 2:
                        bt = filled(dve, ("ptot", n))
                        dve.tensor_tensor(tot, bt[:, 0:H], exn, ALU.add).then_inc(free(("ptot", n)), 1)
                        freed(dve, ("ptot", n))
                        link(dve.reciprocal(tot, tot))
                n = (k - SP_PAIRS - LAG) // SP_PAIRS - 1
                if n >= 0 and (k - SP_PAIRS - LAG) % SP_PAIRS == 3:
                    exn, tot = exn2[:, n % 2, :], tot2[:, n % 2, :]
                    bp = filled(dve, ("pvT", n))
                    for ct in range(2):
                        ins = dve.scalar_tensor_tensor(out=otmp[:, ct, :], in0=exn, scalar=ownv[:, ct, n:n + 1],
                                                       in1=bp[:, ct * H:(ct + 1) * H], op0=ALU.mult, op1=ALU.add)
                    ins.then_inc(free(("pvT", n)), 1)
                    freed(dve, ("pvT", n))
                    for ct in range(2):
                        ins = dve.tensor_tensor(olat[:, ct, n:H * NB:NB], otmp[:, ct, :], tot, ALU.mult)
                    ins.then_inc(olat_ready, 1)
                    dve.wait_ge(olat_ready, n + 1)
            b = filled(dve, "ov")
            dve.tensor_copy(hT[:, 0:H, S:T], b[:, 0:H * NB].rearrange("p (h n) -> p h n", h=H)).then_inc(free("ov"), 1)
            for blk in range(KT):
                for hf in range(2):
                    add_to_stream((("o", 1, blk), hf), blk, hf)
            for blk in range(KT):
                freed(dve, (("o", 1, blk), 1))
            norm(NORM_FFN1, NORM_FFN1, 4)

            def over(v):
                return v.unsqueeze(2).to_broadcast([P, 5, NE])

            b = filled(dve, "rt")
            link(dve.memset(lg, 0.0))
            dve.tensor_copy(lg[:, 0:NT, :], b[:, 0:NT * NE].rearrange("p (a b) -> p a b", a=NT))
            dve.tensor_copy(lg[0:NB, NT, :], b[0:NB, NT * NE:(NT + 1) * NE]).then_inc(free("rt"), 1)
            freed(dve, "rt")
            link(dve.tensor_reduce(lgm, lg, X, ALU.max))
            dve.tensor_tensor(lg, lg, over(lgm), ALU.subtract).then_inc(lg_ready, 1)
            dve.wait_ge(lg_exp, 1)
            link(dve.tensor_reduce(lgs, lg, X, ALU.add))
            link(dve.reciprocal(lgs, lgs))
            link(dve.tensor_tensor(lg, lg, over(lgs), ALU.mult))
            for top, hot in ((top1, oh), (top2, oh2)):
                link(dve.tensor_reduce(top, lg, X, ALU.max))
                link(dve.tensor_tensor(eq, lg, over(top), ALU.is_equal))
                link(dve.tensor_tensor(eq, eq, order.unsqueeze(1).to_broadcast([P, 5, NE]), ALU.mult))
                link(dve.tensor_reduce(tv, eq, X, ALU.max))
                link(dve.tensor_tensor(hot, eq, over(tv), ALU.is_equal))
                if hot is oh:
                    link(dve.scalar_tensor_tensor(out=lg, in0=oh, scalar=-2.0, in1=lg, op0=ALU.mult, op1=ALU.add))
            dve.tensor_tensor(chosen, oh, oh2, ALU.add).then_inc(chosen_ready, 1)
            link(dve.tensor_tensor(tv, top1, top2, ALU.add))
            link(dve.reciprocal(tv, tv))
            link(dve.tensor_tensor(top1, top1, tv, ALU.mult))
            link(dve.tensor_tensor(top2, top2, tv, ALU.mult))
            link(dve.memset(upto1, 0.0))
            link(dve.memset(upto2, 0.0))
            b = filled(dve, "upto")
            count = b[:, (NT + 1) * NE:(NT + 2) * NE]
            link(dve.tensor_scalar(npass, count, 0.0, None, ALU.is_gt))
            for m in range(1, -(-T // SLOTS)):
                link(dve.scalar_tensor_tensor(out=upto1[:, 4:] if m == (T - 1) // SLOTS else npass, in0=count,
                                              scalar=float(m * SLOTS), in1=npass, op0=ALU.is_gt, op1=ALU.add))
            link(dve.tensor_tensor(upto2[:, 4:], upto1[:, 4:], upto1[:, 3:3 + NE], ALU.add))
            link(dve.tensor_tensor(upto1[:, 4:], upto2[:, 4:], upto2[:, 2:2 + NE], ALU.add))
            link(dve.tensor_tensor(upto2[:, 4:], upto1[:, 4:], upto1[:, 0:NE], ALU.add))
            link(dve.tensor_scalar(first, upto2[:, 3:3 + NE], float(SLOTS), -1.0, ALU.mult, ALU.add))
            dve.tensor_tensor(place_of, b[:, 0:5 * NE].rearrange("p (a b) -> p a b", a=5),
                              first.unsqueeze(1).to_broadcast([P, 5, NE]), ALU.add).then_inc(free("upto"), 1)
            freed(dve, "upto")
            for j, hot in enumerate((oh, oh2)):
                link(dve.tensor_tensor(hot, hot, place_of, ALU.mult))
                link(dve.tensor_reduce(slotf[:, j, :], hot, X, ALU.add))
            dve.tensor_copy(slot, slotf).then_inc(slot_ready, 1)
            link(dve.tensor_tensor(cmp[0:1], upto2[0:1, 4:].unsqueeze(1).to_broadcast([1, PASSES, NE]),
                                   numbers[0:1].unsqueeze(2).to_broadcast([1, PASSES, NE]), ALU.is_le))
            link(dve.tensor_reduce(tabf[0:1, 0:PASSES], cmp[0:1], X, ALU.add))
            link(dve.tensor_scalar(tabf[0:1, 0:PASSES], tabf[0:1, 0:PASSES], float(NE - 1), None, ALU.min))
            link(dve.tensor_copy(tabf[0:1, PASSES:PASSES + 1], upto2[0:1, 3 + NE:4 + NE]))
            dve.tensor_copy(table[0:1], tabf[0:1]).then_inc(table_ready, 1)
            dve.wait_ge(table_ready, 1)
            n_passes = dve.value_load(table[0:1, PASSES:PASSES + 1], min_val=1, max_val=PASSES)
            f0, w0, d0 = loops["experts"]
            per = EXPERT_USES
            with dve.Fori(0, PASSES) as p:
                with dve.If(p < n_passes):
                    dve.wait_ge(d_used[DS - 1], p * 2 + d0[DS - 1])
                    for f in range(FB):
                        k, bg, bu = 2 * f + 1, f % 2, 2 + f % 2
                        dve.wait_ge(w_used[k % WS], p * 2 + w0[k % WS] + k // WS + 1)
                        dve.wait_ge(bank_free[bg], p * per[bg] + f0[bg] + f // 2 + 1)
                        dve.tensor_tensor(acte[:, f, :], sge[:, f % 2, :], bank[bu][:, 0:SLOTS], ALU.mult)\
                           .then_inc(bank_free[bu], 1)
                    for i in range(KT):
                        dve.wait_ge(d_used[i % DS], p * 2 + d0[i % DS] + i // DS + 1)
                        dve.tensor_copy(yTe[:, i, :], bank[4 + i % 2][:, 0:SLOTS]).then_inc(bank_free[4 + i % 2], 1)

            dve.wait_ge(back_in, 160)
            dve.wait_ge(gfin_in, 16)
            for t in range(NT + 1):
                n = P if t < NT else NB
                y1, y2 = back[0:n, 2 * t, :], back[0:n, 2 * t + 1, :]
                link(dve.scalar_tensor_tensor(out=y1, in0=y1, scalar=top1[0:n, t:t + 1], in1=xtok2[0:n, t, :],
                                              op0=ALU.mult, op1=ALU.add))
                dve.scalar_tensor_tensor(out=y1, in0=y2, scalar=top2[0:n, t:t + 1], in1=y1,
                                         op0=ALU.mult, op1=ALU.add).then_inc(summed, 1)
            for t in range(NT + 1):
                n = P if t < NT else NB
                y1 = back[0:n, 2 * t, :]
                dve.wait_ge(rooted, t + 1)
                link(dve.reciprocal(outss[0:n, t:t + 1], outss[0:n, t:t + 1]))
                dve.scalar_tensor_tensor(out=y1, in0=y1, scalar=outss[0:n, t:t + 1], in1=gfin[0:n, :],
                                         op0=ALU.mult, op1=ALU.mult).then_inc(normed, 1)

        @block.scalar
        def _(act):
            steps = [0]

            def link(ins):
                steps[0] += 1
                ins.then_inc(act_step, 1)
                act.wait_ge(act_step, steps[0])

            def copy(key, dst, src=None, func=ACT.Copy, scale=1.0):
                b = filled(act, key)
                act.activation(dst, b[:, 0:dst.free_size()] if src is None else src(b), func, scale=scale).then_inc(free(key), 1)

            def squares(ready):
                for kt in range(KT):
                    ready(kt)
                    act.activation(hT[:, kt, :], xT[:, kt, :], ACT.Square).then_inc(sq_done, 1)

            def rms(i, n):
                for hf, (lo, hi) in enumerate(HALVES):
                    b = filled(act, ("ssq", i, hf))
                    act.activation(rstd[:, lo:hi], b[:, 0:HALF], ACT.Sqrt, bias=epst[:, 0:1], scale=1.0 / n)\
                       .then_inc(free(("ssq", i, hf)), 1)

            act.wait_ge(mem_in, 32)
            for t in range(2):
                act.activation(mscr, mtok[:, t, :], ACT.Square, accum_out=memss[:, t:t + 1]).then_inc(mem_sq, 1)
                act.wait_ge(mem_sq, t + 1)
            act.wait_ge(zeros, 3)
            act.activation(memss, memss, ACT.Sqrt, bias=epst[:, 0:1], scale=1.0 / D).then_inc(mem_sq, 1)
            freed(act, "xTs")
            squares(lambda kt: None)
            for l in range(2):
                for blk in range(4):
                    copy((("kv", l, blk), 0), memkT[:, l, blk, :] if blk < 2 else kvT[:, l, blk, :])
                for t in range(2):
                    b = filled(act, ("mtok", l, t))
                    act.activation(mkt[:, l, t, :], b[:, 0:MEM], ACT.Copy)
                    act.activation(memv[:, l, t, :], b[:, MEM:2 * MEM], ACT.Copy).then_inc(free(("mtok", l, t)), 1)
            rms(NORM_MIX0, D)

            def silu(blk):
                act.wait_ge(conv_y, CW * (blk + 1))
                y = Y[:, blk % 2, :]
                act.activation(qkv[:, blk, 0:S], y[:, 0:S], ACT.Silu).then_inc(qkv_ready, 1)
                act.activation(qkv[:, blk, S:T], y[:, S + 3::CW], ACT.Silu).then_inc(qkv_ready, 1)

            for blk in range(QKV + H + 2):
                keys = [(("a", blk), hf) for hf in range(2)]
                if blk < QKV:
                    u = U[:, blk % 2, :]
                    if blk >= 2:
                        act.wait_ge(conv_y, CW * (blk - 1))
                        act.wait_ge(cnew_ready, blk - 1)
                    copy(keys[0], u[:, 3:3 + HALF])
                    b = filled(act, keys[1])
                    act.activation(u[:, 3 + HALF:3 + S], b[:, 0:S - HALF], ACT.Copy)
                    act.activation(u[:, S + 6:UW:CW], b[:, S - HALF:HALF], ACT.Copy).then_inc(free(keys[1]), 1)
                elif blk < QKV + H:
                    for hf, (lo, hi) in enumerate(HALVES):
                        copy(keys[hf], zs[:, blk - QKV, lo:hi], func=ACT.Silu)
                else:
                    for hf, (lo, hi) in enumerate(HALVES):
                        copy(keys[hf], mq0[:, blk - QKV - H, lo:hi])
                if blk == 0:
                    act.wait_ge(gate_in, 1)
                    act.activation(E1, AB, ACT.Exp, scale=-1.0).then_inc(gate_ex, 1)
                    act.wait_ge(gate_ex, 1)
                    act.activation(E1, E1, ACT.Ln, bias=ones[:, 0:1]).then_inc(gate_ex, 1)
                    act.activation(EB, GB[:, :, 0:H], ACT.Exp, scale=-1.0).then_inc(gate_ex, 1)
                    act.activation(EA, alog, ACT.Exp).then_inc(gate_ex, 1)
                if 1 <= blk <= QKV:
                    silu(blk - 1)
                if blk == 5:
                    act.wait_ge(bg_ready, 1)
                    act.activation(egc, BG[:, 0:NT, H:SEL], ACT.Exp).then_inc(egc_ready, 1)
                if blk == 7:
                    b = filled(act, "bgs")
                    act.activation(bsamp.rearrange("p a b -> p (a b)"), b[:, 0:SEL * NB], ACT.Copy)
                    act.activation(egs.rearrange("p a b -> p (a b)"), b[:, H * NB:SEL * NB], ACT.Exp).then_inc(free("bgs"), 1)
            for g in range(5):
                n = min(4, QKV - 4 * g) * P
                if g >= 2:
                    act.wait_ge(co_out[g % 2], 32 * (g // 2))
                b = filled(act, ("cn", g))
                act.activation(cout[0:11, g % 2, 0:n], b[0:11, 0:n], ACT.Copy).then_inc(free(("cn", g)), 1)

            def l2_root(blk):
                q = blk < H
                if blk >= 2:
                    act.wait_ge(l2_done, blk - 1)
                for hf, (lo, hi) in enumerate(HALVES):
                    b = filled(act, ("l2", blk, hf))
                    act.activation(nrb[:, blk % 2, lo:hi], b[:, 0:HALF], ACT.Sqrt, bias=epst[:, 1:2] if q else epst[:, 0:1],
                                   scale=float(HD) if q else 1.0).then_inc(free(("l2", blk, hf)), 1)

            act.wait_ge(conv_y, CW * QKV)
            act.wait_ge(cnew_ready, QKV)
            act.wait_ge(qkv_ready, 2 * QKV)
            for blk in range(2 * H):
                if blk >= 2:
                    filled(act, ("l2", blk - 2, 1))
                act.activation(sqb[:, blk % 2, :], qkv[:, blk, :], ACT.Square).then_inc(l2_sq, 1)
                if blk:
                    l2_root(blk - 1)
            l2_root(2 * H - 1)

            for grp in range(2):
                heads = [3 * grp + i for i in range(3)]
                for i, h in enumerate(heads):
                    b = filled(act, ("row_g", h))
                    if h == 0:
                        act.wait_ge(co_out[0], 96)
                        act.wait_ge(co_out[1], 64)
                    else:
                        act.wait_ge(qg_ready, h)
                        act.wait_ge(glx_ready, h)
                    act.activation(EG, b, ACT.Exp).then_inc(eg_ready, 1)
                    freed(act, ("row_g", h))
                    act.activation(DT, DT, ACT.Exp).then_inc(dt_exp, 1)
                    act.activation(kgs[:, h, :], kgt, ACT.Exp).then_inc(dt_exp, 1)
                for lv in range(LEVELS):
                    for i, h in enumerate(heads):
                        copy(("X", h, lv), Xs[:, i, :])
                for i, h in enumerate(heads):
                    b = filled(act, ("vt", h))
                    for c in range(NT):
                        cc = slice(c * P, (c + 1) * P)
                        ins = act.activation(qkv[:, 2 * H + h, cc], b[:, cc], ACT.Copy, scale=BG[:, c, h:h + 1])
                    ins.then_inc(free(("vt", h)), 1)
                    copy(("wT", h), nWT[:, i, :], scale=-1.0)
                for c in range(NT):
                    for i, h in enumerate(heads):
                        copy(("vn", h, c), vn[:, i, :])

            for g, n in ((0, 4), (1, 2)):
                b = filled(act, ("skt", g))
                act.activation(ktok[0:NB, g * 512:g * 512 + n * P], b[0:NB, 0:n * P], ACT.Copy).then_inc(free(("skt", g)), 1)
            for h in range(H):
                b = filled(act, ("vnt", h))
                act.activation(vnt[0:NB, :], b[0:NB, 0:P], ACT.Copy).then_inc(free(("vnt", h)), 1)

            def head_root(h):
                if h >= 2:
                    act.wait_ge(on_done, h - 1)
                for hf, (lo, hi) in enumerate(HALVES):
                    b = filled(act, ("on", h, hf))
                    act.activation(nrb[:, h % 2, lo:hi], b[:, 0:HALF], ACT.Sqrt, bias=epst[:, 0:1], scale=1.0 / HD)\
                       .then_inc(free(("on", h, hf)), 1)

            for h in range(H):
                freed(act, ("outer", h, 1))
                if h >= 2:
                    filled(act, ("on", h - 2, 1))
                act.activation(sqb[:, h % 2, :], hT[:, h, :], ACT.Square).then_inc(on_sq, 1)
                if h:
                    head_root(h - 1)
            head_root(H - 1)

            def memory_attention(l):
                Pm, PTm, Kb, prod, Vb = mem_bufs[l]

                def exps(m):
                    for j in range(2):
                        act.wait_ge(ms_max, 8 * l + 2 * m + j + 1)
                        if m >= 2:
                            filled(act, ("mpt", l, m - 2, 1))
                        b = filled(act, ("ms", l, m, j))
                        for i in range(2):
                            ins = act.activation(Pm[:, m % 2, 2 * j + i, :], b[:, i * MEM:(i + 1) * MEM], ACT.Exp,
                                                 bias=mmax[:, m, j, i:i + 1], scale=MEM_SCALE, accum_out=msum[:, m, j, i:i + 1])
                        ins.then_inc(free(("ms", l, m, j)), 1)

                exps(0)
                for m in range(MH):
                    if m + 1 < MH:
                        exps(m + 1)
                    for kt in range(2):
                        copy(("mpt", l, m, kt), PTm[:, m % 2, kt, :])
                    if m % 2 == 1:
                        copy(("mo", l, m // 2), hT[:, H + m // 2, 0:S])
                b = filled(act, ("mqs", l))
                act.activation(mqst[0:NB, :], b[0:NB, 0:MEM], ACT.Copy).then_inc(free(("mqs", l)), 1)
                act.wait_ge(m32_max, l + 1)
                b = filled(act, ("mst", l))
                act.activation(Pm32[0:32, :], b[0:32, 0:MEM], ACT.Exp, bias=m32[0:32, :], scale=MEM_SCALE,
                               accum_out=s32[0:32, :]).then_inc(free(("mst", l)), 1)
                copy(("msp", l), pT.rearrange("p a b -> p (a b)"))

            def channel_mixer(name, parts):
                f0, w0, d0 = loops[name]
                per = [8] * 4 + [7] * 4
                with act.Fori(0, parts) as e:
                    for f in range(FB):
                        k = 2 * f
                        act.wait_ge(w_used[k % WS], e * 2 + w0[k % WS] + k // WS + 1)
                        ago, back = (f - 2, 0) if f >= 2 else (FB - 1 - f, 1)
                        for j in (4 * ago + 2, 4 * ago + 3):
                            act.wait_ge(bank_free[j % 8], e * per[j % 8] + f0[j % 8] - back * per[j % 8] + j // 8 + 1)
                        for hf, (lo, hi) in enumerate(HALVES):
                            j = 4 * f + hf
                            act.activation(sg[:, f % 2, lo:hi], bank[j % 8][:, 0:HALF], ACT.Silu).then_inc(bank_free[j % 8], 1)

            act.wait_ge(on_done, H)
            act.wait_ge(sd_out[0], 16 * H // 2)
            act.wait_ge(sd_out[1], 16 * H // 2)
            memory_attention(0)
            filled(act, (("o", 0, KT - 1), 0))
            squares(lambda kt: freed(act, (("o", 0, kt), 1)))
            rms(NORM_FFN0, D)
            channel_mixer("dense", DENSE_PARTS)

            for b in range(8):
                act.wait_ge(bank_free[b], loops["dense"][0][b] + DENSE_PARTS * (8 if b < 4 else 7))
            squares(lambda kt: None)
            rms(NORM_KV, D)
            for blk in range(3):
                for hf, (lo, hi) in enumerate(HALVES):
                    copy((("ckv", blk), hf), raw[:, blk, lo:hi])
            freed(act, (("ckv", 1), 1))
            for j in range(2):
                act.activation(sq1[:, j, :], raw[:, j, :], ACT.Square).then_inc(sq_done, 1)
            for blk in range(5):
                for hf, (lo, hi) in enumerate(HALVES):
                    copy((("b", blk), hf), qlr[:, blk, lo:hi] if blk < 3 else mq1[:, blk - 3, lo:hi])
            act.wait_ge(h_ready, 4 * KT)
            rms("ckv", KV)
            freed(act, (("b", 2), 1))
            for j in range(3):
                act.activation(sq1[:, j, :], qlr[:, j, :], ACT.Square).then_inc(sq_done, 1)
            act.wait_ge(kv_ready, 1)
            rms("ql", QL)
            for h in range(H):
                for hf, (lo, hi) in enumerate(HALVES):
                    copy(("qn", h, hf), qn[:, h, lo:hi])
            for j in range(3):
                for hf, (lo, hi) in enumerate(HALVES):
                    copy(("qp", j, hf), sq1[:, j, lo:hi])
            for h in range(H):
                copy(("kn", h), knT[:, h, :])
            for h in range(H):
                for t in range(NT):
                    n = (t + 1) * P
                    act.wait_ge(at_max, NT * h + t + 1)
                    if h and t == 0:
                        filled(act, ("apt", h - 1, NT - 1))
                    b = filled(act, ("as", h, t))
                    act.activation(Pa[:, t, 0:n], b[:, 0:n], ACT.Exp, bias=atmax[:, h, t:t + 1], scale=MLA_SCALE,
                                   accum_out=atsum[:, h, t:t + 1]).then_inc(free(("as", h, t)), 1)
                for kt in range(NT):
                    copy(("apt", h, kt), PTa[:, kt, kt * P:S], src=lambda b: b[:, kt * P:S])
                copy(("ao", h), hT[:, h, 0:S])
            memory_attention(1)
            for h in range(H):
                copy(("uk", h), wkT[:, h, :])
            def turned(k):
                if k % (GP // 2) == 0:
                    copy(("kpt", k // (GP // 2)), kpT[:, k // (GP // 2) % 2, :])
                if k % 2:
                    copy(("ckt", k), ckT[:, k % (AHEAD + 1), :])

            for k in range(AHEAD):
                turned(k)
            for k in range(PAIRS + SP_PAIRS + LAG + 2):
                if k + AHEAD < PAIRS:
                    turned(k + AHEAD)
                n, at = (k - SP_PAIRS - LAG) // SP_PAIRS - 1, (k - SP_PAIRS - LAG) % SP_PAIRS
                if n >= 0 and at == 1:
                    if n:
                        filled(act, ("pvT", n - 1))
                    copy(("pv", n), pvs[0:H, :], src=lambda b: b[0:H, 0:KV])
                n, at = k // SP_PAIRS - 1, k % SP_PAIRS
                if 0 <= n < NB and at == 4:
                    freed(act, ("sc", n))
                    act.activation(Pp2[:, n % 2, :], Pp2[:, n % 2, :], ACT.Exp, scale=MLA_SCALE).then_inc(pexp_ready, 1)
                    act.activation(exn2[:, n % 2, :], exn2[:, n % 2, :], ACT.Exp, scale=MLA_SCALE).then_inc(pexp_ready, 1)
            filled(act, (("o", 1, KT - 1), 0))
            squares(lambda kt: freed(act, (("o", 1, kt), 1)))
            rms(NORM_FFN1, D)
            act.wait_ge(lg_ready, 1)
            act.activation(lg, lg, ACT.Exp).then_inc(lg_exp, 1)
            act.wait_ge(ck_out, 16 * 10)
            for name, dst in (("ht", htok), ("xt", xtok2)):
                for t in range(NT + 1):
                    n = P if t < NT else NB
                    for j in range(2):
                        b = filled(act, (name, t, j))
                        act.activation(dst[0:n, t, j * 512:(j + 1) * 512], b[0:n, :], ACT.Copy).then_inc(free((name, t, j)), 1)
            for g in range(4):
                copy(("hx", g), hTe[:, 2 * g:2 * g + 2, :].rearrange("p a b -> p (a b)"))
            f0, w0, d0 = loops["experts"]
            per = EXPERT_USES
            act.wait_ge(table_ready, 1)
            n_passes = act.value_load(table[0:1, PASSES:PASSES + 1], min_val=1, max_val=PASSES)
            with act.Fori(0, PASSES) as p:
                with act.If(p < n_passes):
                    for f in range(FB):
                        k, bg, bu = 2 * f, f % 2, 2 + f % 2
                        act.wait_ge(w_used[k % WS], p * 2 + w0[k % WS] + k // WS + 1)
                        act.wait_ge(bank_free[bu], p * per[bu] + f0[bu] + f // 2)
                        act.activation(sge[:, f % 2, :], bank[bg][:, 0:SLOTS], ACT.Silu).then_inc(bank_free[bg], 1)
                    for g in range(4):
                        act.wait_ge(hx, p * 4 + 4 + g + 1)
                        act.activation(hTe[:, 2 * g:2 * g + 2, :].rearrange("p a b -> p (a b)"), bank[6 + g % 2][:, 0:2 * SLOTS],
                                       ACT.Copy).then_inc(bank_free[6 + g % 2], 1)
                    act.wait_ge(rows_out, p * 16 + 16 * ZFILL)
                    for i in range(KT):
                        act.wait_ge(yx, p * KT + i + 1)
                        act.activation(yrow[0:ROWS, :, i * P:(i + 1) * P],
                                       bank[6 + i % 2][0:ROWS, 0:2 * P].rearrange("p (a b) -> p a b", a=2),
                                       ACT.Copy).then_inc(bank_free[6 + i % 2], 1)
            for t in range(NT + 1):
                n = P if t < NT else NB
                act.wait_ge(summed, t + 1)
                act.activation(back[0:n, 2 * t + 1, :], back[0:n, 2 * t, :], ACT.Square, accum_out=outss[0:n, t:t + 1])\
                   .then_inc(out_sq, 1)
                act.wait_ge(out_sq, t + 1)
                act.activation(outss[0:n, t:t + 1], outss[0:n, t:t + 1], ACT.Sqrt, bias=epst[0:n, 0:1], scale=1.0 / D)\
                   .then_inc(rooted, 1)

        @block.gpsimd
        def _(pool):
            pool.memset(GB, 0.0).then_inc(zeros, 1)
            pool.memset(epst[:, 0:1], EPS).then_inc(zeros, 1)
            pool.memset(epst[:, 1:2], EPS * HD).then_inc(zeros, 1)
            mem_out_k = p_mem_k.rearrange("l b (t p) h d -> l (b t) p (h d)", p=P)
            mem_out_v = p_mem_v.rearrange("l b (t p) h d -> l (b t) p (h d)", p=P)
            for l in range(2):
                for t in range(2):
                    freed(pool, ("mtok", l, t))
                    pool.dma_start(mem_out_k[l, t], mkt[:, l, t, :]).then_inc(mem_out, 16)
                    pool.dma_start(mem_out_v[l, t], memv[:, l, t, :]).then_inc(mem_out, 16)
            pool.dma_start(s_conv[0, :, 0:CW - 2, :], a["state_conv"][0, :, 1:CW - 1, :]).then_inc(out_done, 16)

            filled(pool, (("kv", 1, 3), 0))
            freed(pool, ("mtok", 1, 1))
            for i in range(2):
                pool.memset(U[:, i, 0:3], 0.0).then_inc(upad, 1)
            freed(pool, "convw")

            def pad(blk):
                if blk >= 2:
                    pool.wait_ge(conv_y, CW * (blk - 1))
                pool.tensor_copy(U[:, blk % 2, 3 + S:UW].rearrange("p (n w) -> p n w", w=CW)[:, :, 0:CW - 1],
                                 convw[:, blk, 0:24].rearrange("p (n w) -> p n w", w=CW - 1)).then_inc(upad, 1)

            pad(0)
            for blk in range(QKV):
                if blk + 1 < QKV:
                    pad(blk + 1)
                freed(pool, (("a", blk), 1))
                u = U[:, blk % 2, :]
                pool.tensor_copy(cnew[:, blk, 0:3], u[:, S:S + 3])
                pool.tensor_copy(cnew[:, blk, 3:11], u[:, S + 6:UW:CW]).then_inc(cnew_ready, 1)
            for g in range(5):
                n = min(4, QKV - 4 * g) * P
                cols = slice(g * 512, g * 512 + n)
                freed(pool, ("cn", g))
                pool.dma_start(p_conv[0, 0, :, cols], cout[0:3, g % 2, 0:n]).then_inc(co_out[g % 2], 16)
                pool.dma_start(s_conv[0, :, CW - 2, cols], cout[3:11, g % 2, 0:n]).then_inc(co_out[g % 2], 16)

            pool.wait_ge(l2_done, 2 * H)
            pool.wait_ge(mem_out, 128)
            eye4 = ident.unsqueeze(1).to_broadcast([P, NT, P])
            for grp in range(2):
                heads = [3 * grp + i for i in range(3)]
                if grp:
                    filled(pool, ("vn", 2, NT - 1))
                for i, h in enumerate(heads):
                    pool.tensor_copy(Einv[:, i, :].rearrange("p (c i) -> p c i", c=NT), eye4).then_inc(id_ready, 1)
                    pool.tensor_copy(Dinv[:, i, :].rearrange("p (c i) -> p c i", c=NT), eye4).then_inc(id_ready, 1)
                for i, h in enumerate(heads):
                    pool.wait_ge(eg_ready, h + 1)
                    filled(pool, ("qk", h))
                    pool.tensor_tensor(qkv[:, h, 0:S], qkv[:, h, 0:S], EG, ALU.mult).then_inc(qg_ready, 1)
                for i, h in enumerate(heads):
                    freed(pool, ("ds", h, NT - 1))
                    pool.dma_start(p_delta[0, 0, h], St[:, i, :]).then_inc(pd_out, 16)

            freed(pool, ("skt", 1))
            for h in range(H):
                if h:
                    filled(pool, ("outer", h - 1, 1))
                pool.tensor_tensor(kmask[0:NB], ktok[0:NB, h * P:(h + 1) * P].unsqueeze(1).to_broadcast([NB, NB, P]),
                                   ident[0:NB, 0:NB].unsqueeze(2).to_broadcast([NB, NB, P]), ALU.mult).then_inc(kmask_ready, 1)
                freed(pool, ("outer", h, 1))
                pool.dma_start(s_delta[0, :, h].rearrange("n k v -> k n v"),
                               Ssb[:, h % 2, :].rearrange("p (n v) -> p n v", n=NB)).then_inc(sd_out[h % 2], 16)

            freed(pool, ("cktok", 0))
            pool.memset(qps, 0.0).then_inc(zeros, 1)
            pool.memset(zrow, 0.0).then_inc(zeros, 1)
            pool.wait_ge(zeros, 5)
            cells = slots.rearrange("(p a) (b c) -> p (a b) c", p=P, c=ZCOLS)
            per_fill = ZROWS * D // ZCOLS // ZFILL
            for z in range(ZFILL):
                pool.dma_start(cells[:, z * per_fill:(z + 1) * per_fill, :],
                               zrow.unsqueeze(1).to_broadcast([P, per_fill, ZCOLS])).then_inc(rows_out, 16)
            for t in range(NT + 1):
                freed(pool, ("cktok", t))
                if t < NT:
                    pool.dma_start(p_ckv[0, t * P:(t + 1) * P], cktok[:, t, 0:KV]).then_inc(ck_out, 16)
                    pool.dma_start(p_kpe[0, t * P:(t + 1) * P], cktok[:, t, KV:]).then_inc(ck_out, 16)
                else:
                    pool.dma_start(s_ckv.rearrange("n s c -> (n s) c"), cktok[0:NB, t, 0:KV]).then_inc(ck_out, 16)
                    pool.dma_start(s_kpe.rearrange("n s c -> (n s) c"), cktok[0:NB, t, KV:]).then_inc(ck_out, 16)

            pool.wait_ge(page_rows_ready, 2)
            filled(pool, ("mos", 1))
            for G in range(NB * NG):
                if G >= PSLOTS:
                    pool.wait_ge(groups_used, G - PSLOTS + 1)
                elif G == NG:
                    pool.wait_ge(own_prod, 2)
                ckv, kpe = page_slot(G)
                rows_of = bass.IndirectOffsetOnAxis(ap=page_rows[:, G:G + 1], axis=0)
                pool.indirect_dma_start(ckv.rearrange("p g c -> p (g c)"), None,
                                        a["cache_ckv"].rearrange("g (r t) c -> (g r) (t c)", t=GP), rows_of)\
                    .then_inc(pages_in[G % PSLOTS], 16)
                pool.indirect_dma_start(kpe, None, a["cache_kpe"].rearrange("g (r t) c -> (g r) (t c)", t=GP), rows_of)\
                    .then_inc(pages_in[G % PSLOTS], 16)

            pool.wait_ge(rows_out, 16 * ZFILL)
            for t in range(NT + 1):
                for j in range(2):
                    freed(pool, ("ht", t, j))
            pool.wait_ge(slot_ready, 1)
            for t in range(NT + 1):
                n = P if t < NT else NB
                for j in range(2):
                    pool.indirect_dma_start(slots, bass.IndirectOffsetOnAxis(ap=slot[0:n, j, t:t + 1], axis=0),
                                            htok[0:n, t, :], None).then_inc(spread, 16)

            def pass_rows(p):
                return slots[bass.ds(p * SLOTS, SLOTS)].rearrange("(r q) c -> q r c", r=2)

            pool.wait_ge(spread, 160)
            pool.dma_start(hrow[0:ROWS], slots[0:SLOTS].rearrange("(r q) c -> q r c", r=2)).then_inc(hrow_in, 16)
            f0, w0, d0 = loops["experts"]
            per = EXPERT_USES
            pool.wait_ge(table_ready, 1)
            n_passes = pool.value_load(table[0:1, PASSES:PASSES + 1], min_val=1, max_val=PASSES)
            with pool.Fori(0, PASSES) as p:
                with pool.If(p < n_passes):
                    pool.wait_ge(hx, p * 4 + 4)
                    pool.dma_start(hrow[0:ROWS], pass_rows(p + 1)).then_inc(hrow_in, 16)
                    for bk in (6, 7):
                        pool.wait_ge(bank_free[bk], p * per[bk] + f0[bk] + per[bk])
                    pool.dma_start(pass_rows(p), yrow[0:ROWS]).then_inc(rows_out, 16)
                    pool.wait_ge(rows_out, p * 16 + 16 * (ZFILL + 1))
            for t in range(NT + 1):
                n = P if t < NT else NB
                for j in range(2):
                    pool.indirect_dma_start(back[0:n, 2 * t + j, :], None, slots,
                                            bass.IndirectOffsetOnAxis(ap=slot[0:n, j, t:t + 1], axis=0)).then_inc(back_in, 16)
            for t in range(NT + 1):
                pool.wait_ge(normed, t + 1)
                if t < NT:
                    pool.dma_start(y_prompt[0, t * P:(t + 1) * P], back[:, 2 * t, :]).then_inc(out_done, 16)
                else:
                    pool.dma_start(y_sample.rearrange("n s c -> (n s) c"), back[0:NB, 2 * t, :]).then_inc(out_done, 16)
            pool.wait_ge(mem_out, 128)
            pool.wait_ge(co_out[0], 96)
            pool.wait_ge(co_out[1], 64)
            pool.wait_ge(pd_out, 16 * H)
            pool.wait_ge(sd_out[0], 16 * H // 2)
            pool.wait_ge(sd_out[1], 16 * H // 2)
            pool.wait_ge(ck_out, 16 * 10)
            pool.wait_ge(out_done, 16 * (1 + 5))

        @block.sync
        def _(sp):
            def load(dst, src, signal):
                sp.dma_start(dst, src).then_inc(signal, 16)

            def rows(w):
                return w.rearrange("(k p) c -> p k c", p=P)

            load(CF, a["const_f32"][0:P, :], consts_in)
            load(sel, a["const_sel"].rearrange("r (q p) -> r q p", q=SEL), consts_in)
            for t in range(2):
                load(mtok[:, t, :], a["mem_prompt"][0, t * P:(t + 1) * P, :], mem_in)
            load(gtok[0:2, :], a["g_mix"], rows_in)
            load(gtok[2:4, :], a["g_ffn"], rows_in)
            load(gtok[4:5, :], a["g_final"].unsqueeze(0), rows_in)
            load(gtok[5:6, :], a["g_kv"].unsqueeze(0), rows_in)
            load(gtok[6:8, :], a["g_mem"], rows_in)
            for t in range(NT):
                load(xtok[:, t, :], a["x_prompt"][0, t * P:(t + 1) * P, :], x_in)
            load(xtok[0:NB, NT, :], a["x_sample"].rearrange("n s c -> (n s) c"), x_in)
            load(cvtok[0:24, :], a["state_conv"][0].rearrange("n w c -> (n w) c"), conv_in)
            load(cvtok[24:28, :], a["conv_w"][0], conv_in)

            def weights(keys):
                for key in keys:
                    at, s, n = w_order.pop(0)
                    assert at == key
                    if n:
                        sp.wait_ge(w_used[s], n)
                    dst = w_ring[:, s, :, :]
                    kind, blk = key[0], key[-1]
                    c = slice(blk * P, (blk + 1) * P)
                    if kind == "kv":
                        load(dst, rows(a["w_mem_kv"][key[1]])[:, :, c], w_loaded[s])
                    elif kind == "a":
                        at = blk * P if blk < QKV + H else IN_A - MEM + (blk - QKV - H) * P
                        load(dst, rows(a["w_in_a"][0])[:, :, at:at + P], w_loaded[s])
                    elif kind == "o":
                        load(dst, rows(a["w_out"][key[1]])[:, :, c], w_loaded[s])
                    elif kind == "ckv" and blk < 2:
                        load(dst, rows(a["w_kv_a"])[:, :, c], w_loaded[s])
                    elif kind == "ckv":
                        w = rows(a["w_kv_a"])[:, :, KV:KV + ROPE]
                        sp.dma_start(dst[:, :, 0:ROPE], w).then_inc(half_in, 16)
                        sp.wait_ge(half_in, 16)
                        load(dst[:, :, ROPE:P], w, w_loaded[s])
                    else:
                        load(dst, rows(a["w_in_b"][0])[:, :, c], w_loaded[s])

            weights([("kv", 0, i) for i in range(4)])
            load(lmw.bitcast(I32), a["const_masks"], masks_in)
            load(wba, rows(a["w_in_a"][0])[:, :, CONV + H * HD:CONV + H * HD + SEL], small_in)
            load(wrt, rows(a["w_router"][0]), small_in)
            sp.dma_start(g_on, a["g_onorm"].rearrange("l p -> p l"),
                         allow_slow_non_contiguous=True).then_inc(small_in, 16)
            sp.dma_start(g_ql, a["g_qlora"][0].rearrange("(k p) -> p k", p=P),
                         allow_slow_non_contiguous=True).then_inc(small_in, 16)
            sp.dma_start(g_ck, a["g_ckv"].rearrange("(k p) -> p k", p=P),
                         allow_slow_non_contiguous=True).then_inc(small_in, 16)
            load(alog, a["a_log"].partition_broadcast(P).rearrange("p l h -> p (l h)"), small_in)
            load(dtb, a["dt_bias"].partition_broadcast(P).rearrange("p l h -> p (l h)"), small_in)
            for j in range(GP):
                sp.dma_start(page_rows[j * P // GP:(j + 1) * P // GP, :],
                             a["page_table"].rearrange("n (g j) -> j (n g)", j=GP)[j].partition_broadcast(P // GP),
                             allow_slow_non_contiguous=True).then_inc(table_in, 16)
            weights([("kv", 1, i) for i in range(4)])
            weights([("a", i) for i in range(QKV + H + 2)])
            weights([("o", 0, i) for i in range(KT)])
            freed(sp, ("ds", H - 1, NT - 1))
            sp.wait_ge(pd_out, 16 * H)
            for h in range(H):
                if h >= 2:
                    sp.wait_ge(sd_out[h % 2], 16 * (h // 2))
                load(Ssb[:, h % 2, :].rearrange("p (n v) -> p n v", n=NB),
                     a["state_delta"][0, :, h].rearrange("n k v -> k n v"), states_in[h % 2])

            def memory_rows(l):
                Pm, PTm, Kb, prod, Vb = mem_bufs[l]
                ck = a["cache_mem_k"][l].rearrange("n (t p) h d -> n p t (h d)", p=P)
                cv = a["cache_mem_v"][l].rearrange("n (t p) h d -> n p t (h d)", p=P)
                for n in range(NB):
                    if n >= 2:
                        sp.wait_ge(kb_used, NB * l + n - 1)
                    load(Kb[:, n % 2], ck[n], kb_in[n % 2])
                    load(Vb[:, n], cv[n], v_in)

            def channel_mixer(name, parts, wg, wu, wd):
                f0, w0, d0 = loops[name]
                with sp.Fori(0, parts) as e:
                    for k in range(2 * FB):
                        s, r = k % WS, k // WS
                        sp.wait_ge(w_used[s], e * 2 + w0[s] + r)
                        load(w_ring[:, s, :, :], (wu if k % 2 else wg)(e, k // 2), w_loaded[s])
                    for i in range(KT):
                        s, r = i % DS, i // DS
                        sp.wait_ge(d_used[s], e * 2 + d0[s] + r)
                        load(d_ring[:, s, :].rearrange("p (f c) -> p f c", f=FB), wd(e, i), d_loaded[s])

            sp.wait_ge(on_done, H)
            for i in range(2):
                sp.wait_ge(sd_out[i], 16 * H // 2)
            memory_rows(0)
            filled(sp, ("mos", 0))
            channel_mixer("dense", DENSE_PARTS,
                          lambda e, f: rows(a["w_gate"][0])[:, :, bass.ds(e * FE + f * P, P)],
                          lambda e, f: rows(a["w_up"][0])[:, :, bass.ds(e * FE + f * P, P)],
                          lambda e, i: a["w_down"][0][bass.ds(e * FE, FE), i * P:(i + 1) * P].rearrange("(f p) c -> p f c", p=P))
            weights([("ckv", i) for i in range(3)] + [("b", i) for i in range(5)])
            sp.wait_ge(d_used[DS - 1], loops["dense"][2][DS - 1] + 2 * DENSE_PARTS)
            load(cs, a["const_rope"].rearrange("p (a t) -> p a t", a=2), rope_in)
            wq = a["w_q_b"][0].rearrange("(k p) (h c) -> p k h c", p=P, h=H)
            for kt in range(3):
                load(wqn[:, kt, :].rearrange("p (h c) -> p h c", h=H), wq[:, kt, :, 0:HD], wq_in)
                load(wqp[:, kt, :].rearrange("p (h c) -> p h c", h=H), wq[:, kt, :, HD:QH], wq_in)
            load(wuk, a["w_uk"].rearrange("(k p) h c -> p k (h c)", p=P), wkv_in)
            load(wuv, a["w_uv"].rearrange("(k p) h c -> p k (h c)", p=P), wkv_in)
            weights([("o", 1, i) for i in range(KT)])
            filled(sp, ("ao", H - 1))
            memory_rows(1)
            filled(sp, ("mos", 1))
            filled(sp, "ov")
            sp.wait_ge(rows_out, 16 * ZFILL)
            sp.wait_ge(ck_out, 16 * 10)
            load(gfin, a["g_final"].partition_broadcast(P), gfin_in)
            f0, w0, d0 = loops["experts"]
            sp.wait_ge(table_ready, 1)
            n_passes = sp.value_load(table[0:1, PASSES:PASSES + 1], min_val=1, max_val=PASSES)
            with sp.Fori(0, PASSES) as p:
                with sp.If(p < n_passes):
                    e = sp.value_load(table[0:1, bass.ds(p, 1)], min_val=0, max_val=NE - 1)
                    for k in range(2 * FB):
                        s, r = k % WS, k // WS
                        sp.wait_ge(w_used[s], p * 2 + w0[s] + r)
                        w = a["we_up" if k % 2 else "we_gate"][0][bass.ds(e, 1), :, k // 2 * P:(k // 2 + 1) * P]
                        load(w_ring[:, s, :, :], w.rearrange("a (k p) c -> p (a k) c", p=P), w_loaded[s])
                    for i in range(KT):
                        s, r = i % DS, i // DS
                        sp.wait_ge(d_used[s], p * 2 + d0[s] + r)
                        w = a["we_down"][0][bass.ds(e, 1), :, i * P:(i + 1) * P]
                        load(d_ring[:, s, :].rearrange("p (f c) -> p f c", f=FB), w.rearrange("a (f p) c -> p (a f) c", p=P),
                             d_loaded[s])


_INS = ['x_prompt', 'x_sample', 'cache_mem_k', 'cache_mem_v', 'cache_ckv', 'cache_kpe', 'state_delta', 'state_conv',
        'page_table', 'mem_prompt', 'g_mix', 'g_ffn', 'g_final', 'w_in_a', 'conv_w', 'a_log', 'dt_bias', 'g_onorm',
        'w_in_b', 'g_qlora', 'w_q_b', 'g_kv', 'w_kv_a', 'g_ckv', 'w_uk', 'w_uv', 'g_mem', 'w_mem_kv', 'w_out',
        'w_gate', 'w_up', 'w_down', 'w_router', 'we_gate', 'we_up', 'we_down']
_OUTS = [(1, S, D), (NB, 1, D), (1, 1, H, HD, HD), (1, 1, CW - 1, CONV), (1, S, KV), (1, S, ROPE),
         (2, 1, MEM, MH, MD), (2, 1, MEM, MH, MD), (1, NB, H, HD, HD), (1, NB, CW - 1, CONV), (NB, 1, KV), (NB, 1, ROPE)]


def constants():
    import numpy as np
    i = np.arange(P)
    f = np.zeros((P, 5 * P + NE + PASSES + 1), np.float32)
    f[:, 0:P] = np.eye(P)
    f[:, P:2 * P] = 1.0
    f[:, 2 * P:3 * P] = i[:, None] <= i[None, :]
    f[:, 3 * P:4 * P] = np.where(i[None, :] <= i[:, None], 0.0, NEG)
    for base in (0, ROPE):
        for m in range(ROPE // 2):
            f[base + m + ROPE // 2, 4 * P + base + m] = -1.0
            f[base + m, 4 * P + base + m + ROPE // 2] = 1.0
    f[:, 5 * P:5 * P + NE] = NE - np.arange(NE)
    f[:, 5 * P + NE:-1] = np.arange(PASSES)
    f[:, -1] = i % (P // GP)
    sel = np.zeros((SEL, SEL, P), np.float32)
    for r in range(SEL):
        sel[r, r] = 1.0
    masks = np.zeros((P, 2 * LEVELS, P), np.uint8)
    for lv in range(LEVELS):
        s = 1 << lv
        lower = (i[:, None] // s % 2 == 1) & (i[None, :] // s == i[:, None] // s - 1)
        masks[:, lv] = lower
        masks[:, LEVELS + lv] = lower.T
    half = ROPE // 2
    inv = np.float32(10000.0) ** (-np.arange(half, dtype=np.float32) / np.float32(half))
    pos = np.concatenate([np.arange(S), np.full(NB, PAGES * P)]).astype(np.float32)
    ang = (pos[:, None] * inv.astype(np.float32)[None, :]).astype(np.float32).T
    cos, sin = np.tile(np.cos(ang), (4, 1)), np.tile(np.sin(ang), (4, 1))
    rope = np.concatenate([cos, sin], 1).astype(np.float32)
    return {"const_f32": f, "const_sel": sel.reshape(SEL, -1), "const_masks": masks.reshape(P, -1).view(np.int32), "const_rope": rope}


def kernel(**inputs):
    import numpy as np
    import concourse.bacc as bacc
    from concourse.bass_utils import run_bass_kernel_spmd

    nc = bacc.Bacc("TRN2", target_bir_lowering=False, num_devices=1)
    arrays = {f"in_{n}": np.ascontiguousarray(inputs[n]) for n in _INS}
    arrays.update({f"in_{n}": v for n, v in constants().items()})
    aps = {n[3:]: nc.dram_tensor(n, v.shape, mybir.dt.from_np(v.dtype), kind="ExternalInput").ap() for n, v in arrays.items()}
    outs = [nc.dram_tensor(f"out_{i}", s, F32, kind="ExternalOutput").ap() for i, s in enumerate(_OUTS)]
    build(nc, aps, outs)
    r = run_bass_kernel_spmd(nc, [arrays], core_ids=[0])
    return tuple(r.results[0][f"out_{i}"] for i in range(len(_OUTS)))
```
